# Optimizing a Trainium2 kernel written in Bass

```python
import math
import jax
import jax.numpy as jnp
from jax import lax
import numpy as np

D_MODEL = 1024
BATCH = 1
SEQ = 256
DEPTH = 2

MIX_W = D_MODEL
GROUP_W = MIX_W // 2
N_EVEN = (DEPTH + 1) // 2
N_ODD = DEPTH // 2
RMS_EPS = 1e-6
D_FF = 2816

HG_HEADS = 4
HG_DK = GROUP_W // HG_HEADS
HG_DV = GROUP_W // HG_HEADS
HG_CHUNK = 32
SC_CH = GROUP_W
CONV_W = 3
ML_HEADS = 4
ML_DH = GROUP_W // ML_HEADS
ML_CHUNK = 64
MB_HEADS = 4
MB_DH = GROUP_W // MB_HEADS
MB_BLOCK = 256
MB_TOPK = 3
MB_QCHUNK = 64
ROPE_THETA = 500000.0
ROPE_DIM = MB_DH // 4

AB_IN = 4 * GROUP_W + 3 * SC_CH
CD_IN = 4 * GROUP_W + 2 * ML_HEADS + 3 * GROUP_W

kernel_name = "hybrid_hgrn2_shortconv_mlstm_moba_macaron"

def rms_norm(x, gain):
    xf = x.astype(jnp.float32)
    y = xf * lax.rsqrt(jnp.mean(xf * xf, axis=-1, keepdims=True) + RMS_EPS)
    return (y * gain.astype(jnp.float32)).astype(x.dtype)

def swiglu(x, w_in, w_out):
    gate, up = jnp.split(x @ w_in, 2, axis=-1)
    return (jax.nn.silu(gate) * up) @ w_out

def split_heads(t, n_heads):
    return t.reshape(t.shape[0], t.shape[1], n_heads, -1)

def to_chunks(t, chunk):
    b, s = t.shape[0], t.shape[1]
    return jnp.moveaxis(t.reshape(b, s // chunk, chunk, *t.shape[2:]), 3, 1)

def from_chunks(t):
    b, h, nc, l, d = t.shape
    return jnp.moveaxis(t, 1, 3).reshape(b, nc * l, h, d)

def hgrn2_heads(q, f_pre, i_in, lb):
    f = lb + (1.0 - lb) * jax.nn.sigmoid(f_pre)
    qc = to_chunks(jax.nn.silu(q), HG_CHUNK)
    kc = to_chunks(1.0 - f, HG_CHUNK)
    vc = to_chunks(i_in, HG_CHUNK)
    b = jnp.cumsum(to_chunks(jnp.log(f), HG_CHUNK), axis=3)
    b_end = b[:, :, :, -1:, :]
    q_dec = qc * jnp.exp(b)
    k_dec = kc * jnp.exp(-b)
    causal = jnp.tril(jnp.ones((HG_CHUNK, HG_CHUNK), dtype=bool))
    attn = jnp.where(causal, jnp.einsum('bhcid,bhcjd->bhcij', q_dec, k_dec), 0.0)
    o_intra = jnp.einsum('bhcij,bhcjv->bhciv', attn, vc)
    d_state = jnp.einsum('bhcjd,bhcjv->bhcdv', kc * jnp.exp(b_end - b), vc)
    decay = jnp.exp(b_end[:, :, :, 0, :])

    def step(state, xs):
        dec, ds = xs
        return dec[..., None] * state + ds, state

    s0 = jnp.zeros(d_state.shape[:2] + d_state.shape[3:], d_state.dtype)
    _, s_prev = lax.scan(step, s0, (jnp.moveaxis(decay, 2, 0), jnp.moveaxis(d_state, 2, 0)))
    s_prev = jnp.moveaxis(s_prev, 0, 2)
    o = o_intra + jnp.einsum('bhcid,bhcdv->bhciv', q_dec, s_prev)
    return from_chunks(o)

def short_conv_channels(b_gate, c_gate, u, conv_w, conv_b):
    z = c_gate * u
    s = z.shape[1]
    zp = jnp.pad(z, ((0, 0), (CONV_W - 1, 0), (0, 0)))
    y = conv_b + sum(conv_w[j] * zp[:, j:j + s] for j in range(CONV_W))
    return b_gate * y

def mlstm_heads(q, k, v, log_i, log_f):
    qc, kc, vc = (to_chunks(t, ML_CHUNK) for t in (q, k, v))
    ic = to_chunks(log_i, ML_CHUNK)
    b = jnp.cumsum(to_chunks(log_f, ML_CHUNK), axis=-1)
    b_end = b[..., -1]
    causal = jnp.tril(jnp.ones((ML_CHUNK, ML_CHUNK), dtype=bool))
    d_log = jnp.where(causal, b[..., :, None] - b[..., None, :] + ic[..., None, :], -jnp.inf)
    w_end = b_end[..., None] - b + ic
    m_end = jnp.max(w_end, axis=-1)

    def step(carry, xs):
        c_mat, n_vec, m = carry
        k_c, v_c, w_c, m_c, be = xs
        m_new = jnp.maximum(be + m, m_c)
        a = jnp.exp(be + m - m_new)
        wk = jnp.exp(w_c - m_new[..., None])[..., None] * k_c
        c_new = a[..., None, None] * c_mat + jnp.einsum('bhld,bhle->bhde', wk, v_c)
        n_new = a[..., None] * n_vec + wk.sum(axis=-2)
        return (c_new, n_new, m_new), (c_mat, n_vec, m)

    bsz, n_h, dh = q.shape[0], q.shape[2], q.shape[3]
    init = (jnp.zeros((bsz, n_h, dh, dh), q.dtype), jnp.zeros((bsz, n_h, dh), q.dtype),
            jnp.zeros((bsz, n_h), q.dtype))
    xs = tuple(jnp.moveaxis(t, 2, 0) for t in (kc, vc, w_end, m_end, b_end))
    _, (c_prev, n_prev, m_prev) = lax.scan(step, init, xs)
    c_prev = jnp.moveaxis(c_prev, 0, 2)
    n_prev = jnp.moveaxis(n_prev, 0, 2)
    m_prev = jnp.moveaxis(m_prev, 0, 2)
    log_inter = b + m_prev[..., None]
    m_t = jnp.maximum(log_inter, jnp.max(d_log, axis=-1))
    weights = jnp.exp(d_log - m_t[..., None]) * jnp.einsum('bhcid,bhcjd->bhcij', qc, kc)
    a_in = jnp.exp(log_inter - m_t)
    num = jnp.einsum('bhcij,bhcje->bhcie', weights, vc) + a_in[..., None] * jnp.einsum('bhcid,bhcde->bhcie', qc, c_prev)
    den = weights.sum(axis=-1) + a_in * jnp.einsum('bhcid,bhcd->bhci', qc, n_prev)
    h = num / jnp.maximum(jnp.abs(den), jnp.exp(-m_t))[..., None]
    return from_chunks(h)

def rope_partial(x, pos):
    half = ROPE_DIM // 2
    inv_freq = jnp.float32(ROPE_THETA) ** (-jnp.arange(half, dtype=jnp.float32) * 2.0 / ROPE_DIM)
    ang = pos.astype(jnp.float32)[:, None] * inv_freq[None, :]
    cos = jnp.cos(ang)[None, :, None, :]
    sin = jnp.sin(ang)[None, :, None, :]
    x1, x2, x_pass = x[..., :half], x[..., half:ROPE_DIM], x[..., ROPE_DIM:]
    return jnp.concatenate([x1 * cos - x2 * sin, x2 * cos + x1 * sin, x_pass], axis=-1)

def moba_heads(q, k, v):
    bsz, s, n_h, dh = q.shape
    s_pad = -(-s // MB_BLOCK) * MB_BLOCK
    n_blk = s_pad // MB_BLOCK
    n_sel = min(MB_TOPK, n_blk)
    padw = ((0, 0), (0, s_pad - s), (0, 0), (0, 0))
    q, k, v = (jnp.pad(t, padw).transpose(0, 2, 1, 3) for t in (q, k, v))
    k_blk = k.reshape(bsz, n_h, n_blk, MB_BLOCK, dh)
    v_blk = v.reshape(bsz, n_h, n_blk, MB_BLOCK, dh)
    k_mean = k_blk.mean(axis=3)
    n_qc = s_pad // MB_QCHUNK
    q_chunks = jnp.moveaxis(q.reshape(bsz, n_h, n_qc, MB_QCHUNK, dh), 2, 0)
    b_idx = jnp.arange(bsz)[:, None, None, None]
    h_idx = jnp.arange(n_h)[None, :, None, None]
    blk_ids = jnp.arange(n_blk)

    def attend(args):
        c, q_c = args
        q_pos = c * MB_QCHUNK + jnp.arange(MB_QCHUNK)
        own = (c * MB_QCHUNK) // MB_BLOCK
        gate = jnp.einsum('bhqd,bhnd->bhqn', q_c, k_mean)
        gate = jnp.where(blk_ids < own, gate, -jnp.inf)
        g_val, sel = lax.top_k(gate, n_sel)
        sel_ok = jnp.isfinite(g_val)
        k_sel = k_blk[b_idx, h_idx, sel]
        v_sel = v_blk[b_idx, h_idx, sel]
        s_past = jnp.einsum('bhqd,bhqnld->bhqnl', q_c, k_sel)
        s_past = jnp.where(sel_ok[..., None], s_past, -jnp.inf).reshape(bsz, n_h, MB_QCHUNK, n_sel * MB_BLOCK)
        k_own = lax.dynamic_index_in_dim(k_blk, own, axis=2, keepdims=False)
        v_own = lax.dynamic_index_in_dim(v_blk, own, axis=2, keepdims=False)
        k_pos = own * MB_BLOCK + jnp.arange(MB_BLOCK)
        s_own = jnp.where(k_pos[None, :] <= q_pos[:, None], jnp.einsum('bhqd,bhld->bhql', q_c, k_own), -jnp.inf)
        p = jax.nn.softmax(jnp.concatenate([s_past, s_own], axis=-1), axis=-1)
        p_past = p[..., :n_sel * MB_BLOCK].reshape(bsz, n_h, MB_QCHUNK, n_sel, MB_BLOCK)
        p_own = p[..., n_sel * MB_BLOCK:]
        return jnp.einsum('bhqnl,bhqnld->bhqd', p_past, v_sel) + jnp.einsum('bhql,bhld->bhqd', p_own, v_own)

    out = lax.map(attend, (jnp.arange(n_qc), q_chunks))
    out = jnp.moveaxis(out, 0, 2).reshape(bsz, n_h, s_pad, dh)[:, :, :s]
    return out.transpose(0, 2, 1, 3)

def mixer_ab(h, w_in, w_out, lb, hg_norm, conv_w, conv_b):
    proj = (h @ w_in).astype(jnp.float32)
    q, f_pre, i_in, g, sc_b, sc_c, sc_u = jnp.split(proj, 7, axis=-1)
    o = hgrn2_heads(split_heads(q, HG_HEADS), split_heads(f_pre, HG_HEADS),
                    split_heads(i_in, HG_HEADS), lb.reshape(HG_HEADS, HG_DK))
    o = rms_norm(o, hg_norm) * jax.nn.silu(split_heads(g, HG_HEADS))
    y_hg = o.reshape(h.shape[0], h.shape[1], GROUP_W)
    y_sc = short_conv_channels(sc_b, sc_c, sc_u, conv_w, conv_b)
    return jnp.concatenate([y_hg, y_sc], axis=-1).astype(h.dtype) @ w_out

def mixer_cd(h, w_in, w_out, gate_bias, ml_norm):
    bsz, s = h.shape[0], h.shape[1]
    proj = (h @ w_in).astype(jnp.float32)
    ml_q, ml_k, ml_v, ml_o = jnp.split(proj[..., :4 * GROUP_W], 4, axis=-1)
    gates = proj[..., 4 * GROUP_W:4 * GROUP_W + 2 * ML_HEADS]
    mb_q, mb_k, mb_v = jnp.split(proj[..., 4 * GROUP_W + 2 * ML_HEADS:], 3, axis=-1)
    log_i = gates[..., :ML_HEADS] + gate_bias[0]
    log_f = jax.nn.log_sigmoid(gates[..., ML_HEADS:] + gate_bias[1])
    h_ml = mlstm_heads(split_heads(ml_q, ML_HEADS) * ML_DH ** -0.5, split_heads(ml_k, ML_HEADS),
                       split_heads(ml_v, ML_HEADS), log_i, log_f)
    h_ml = rms_norm(h_ml, ml_norm) * jax.nn.sigmoid(split_heads(ml_o, ML_HEADS))
    pos = jnp.arange(s)
    y_mb = moba_heads(rope_partial(split_heads(mb_q, MB_HEADS), pos) * MB_DH ** -0.5,
                      rope_partial(split_heads(mb_k, MB_HEADS), pos), split_heads(mb_v, MB_HEADS))
    y = jnp.concatenate([h_ml.reshape(bsz, s, GROUP_W), y_mb.reshape(bsz, s, GROUP_W)], axis=-1)
    return y.astype(h.dtype) @ w_out

def setup_inputs(seed: int = 0) -> dict:
    key = jax.random.key(seed)
    ks = jax.random.split(key, 17)

    def dense(k, shape, fan_in):
        return jax.random.normal(k, shape, jnp.float32) * fan_in ** -0.5

    def gain(k, shape):
        return 1.0 + 0.02 * jax.random.normal(k, shape, jnp.float32)

    gate_bias = jnp.stack([0.1 * jax.random.normal(ks[13], (N_ODD, ML_HEADS), jnp.float32),
                           jnp.linspace(3.0, 6.0, ML_HEADS, dtype=jnp.float32)[None, :]
                           + 0.1 * jax.random.normal(ks[14], (N_ODD, ML_HEADS), jnp.float32)], axis=1)
    return {
        "x": jax.random.normal(ks[0], (BATCH, SEQ, D_MODEL), jnp.float32),
        "ffn_norm": gain(ks[1], (DEPTH, 2, D_MODEL)),
        "ffn_w_in": dense(ks[2], (DEPTH, 2, D_MODEL, 2 * D_FF), D_MODEL),
        "ffn_w_out": dense(ks[3], (DEPTH, 2, D_FF, D_MODEL), D_FF),
        "mix_norm": gain(ks[4], (DEPTH, D_MODEL)),
        "ab_w_in": dense(ks[5], (N_EVEN, D_MODEL, AB_IN), D_MODEL),
        "ab_w_out": dense(ks[6], (N_EVEN, MIX_W, D_MODEL), MIX_W),
        "hgrn_lb_logits": 0.1 * jax.random.normal(ks[7], (DEPTH + 1, HG_HEADS * HG_DK), jnp.float32),
        "hgrn_out_norm": gain(ks[8], (N_EVEN, HG_HEADS, HG_DV)),
        "conv_w": dense(ks[9], (N_EVEN, CONV_W, SC_CH), CONV_W),
        "conv_b": 0.02 * jax.random.normal(ks[10], (N_EVEN, SC_CH), jnp.float32),
        "cd_w_in": dense(ks[11], (N_ODD, D_MODEL, CD_IN), D_MODEL),
        "cd_w_out": dense(ks[12], (N_ODD, MIX_W, D_MODEL), MIX_W),
        "mlstm_gate_bias": gate_bias,
        "mlstm_out_norm": gain(ks[15], (N_ODD, ML_HEADS, ML_DH)),
        "final_norm": gain(ks[16], (D_MODEL,)),
    }

def reference(x, ffn_norm, ffn_w_in, ffn_w_out, mix_norm, ab_w_in, ab_w_out, hgrn_lb_logits,
              hgrn_out_norm, conv_w, conv_b, cd_w_in, cd_w_out, mlstm_gate_bias, mlstm_out_norm,
              final_norm):
    lower_bounds = jnp.cumsum(jax.nn.softmax(hgrn_lb_logits.astype(jnp.float32), axis=0), axis=0)
    for layer in range(DEPTH):
        x = x + 0.5 * swiglu(rms_norm(x, ffn_norm[layer, 0]), ffn_w_in[layer, 0], ffn_w_out[layer, 0])
        h = rms_norm(x, mix_norm[layer])
        if layer % 2 == 0:
            e = layer // 2
            x = x + mixer_ab(h, ab_w_in[e], ab_w_out[e], lower_bounds[layer], hgrn_out_norm[e],
                             conv_w[e], conv_b[e])
        else:
            o = layer // 2
            x = x + mixer_cd(h, cd_w_in[o], cd_w_out[o], mlstm_gate_bias[o], mlstm_out_norm[o])
        x = x + 0.5 * swiglu(rms_norm(x, ffn_norm[layer, 1]), ffn_w_in[layer, 1], ffn_w_out[layer, 1])
    return rms_norm(x, final_norm)


_drawn_inputs = setup_inputs


def setup_inputs(seed=0):
    import zlib

    import numpy as np

    out = dict(_drawn_inputs(seed))
    spreads = {}
    factors = {'ffn_norm': 3.174,
     'hgrn_lb_logits': 8.0,
     'hgrn_out_norm': 7.911,
     'conv_b': 4.3,
     'mlstm_out_norm': 8.0,
     'final_norm': 2.861}
    for name, (base, spread) in spreads.items():
        noise = np.random.default_rng([zlib.crc32(name.encode()), seed]).standard_normal(out[name].shape)
        drawn = base * np.exp(spread * noise) if base else spread * noise
        out[name] = jnp.asarray(drawn.astype(out[name].dtype))
    for name, factor in factors.items():
        out[name] = (out[name] * factor).astype(out[name].dtype)
    return out
```

```python
from contextlib import ExitStack

import numpy as np

import concourse.bass as bass
from concourse import mybir

F32 = mybir.dt.float32
F32R = mybir.dt.float32r
BF16 = mybir.dt.bfloat16
ALU = mybir.AluOpType
ACT = mybir.ActivationFunctionType
AX = mybir.AxisListType

P = 128
D = 1024
S = 256
T = S // P
KD = D // P
F = 2816
G = 512
H = G // P
PAIR = 2 * P
SLOT = KD * PAIR
ITER = F // PAIR
RING = 3
NMIX = 18
HGC = 32
EPS = 1e-6
MASKED = -1e30

FFN_BASE = [0, 3 * ITER + NMIX, 6 * ITER + NMIX, 9 * ITER + 2 * NMIX]
MIX_BASE = [3 * ITER, 9 * ITER + NMIX]
SLOTS = 12 * ITER + 2 * NMIX
OUT_FFN = [0, ITER + 4, 2 * ITER + 4, 3 * ITER + 8]
OUT_MIX = [ITER, 3 * ITER + 4]
PHASES = [("ffn", 0), ("ab", 0), ("ffn", 1), ("ffn", 2), ("cd", 1), ("ffn", 3)]
CHUNKS = 28

C_FFN, C_MIX, C_HGN, C_CW, C_CB, C_MLN, C_LB, N_ROWS = 0, 32, 48, 52, 64, 68, 72, 84

CONST = dict(ident=128, ones=128, m_ij=384, m_ji=384, bd=128, reset=256, cos=256, sin=256, rot=128, sel=512)
C_AT = {}
for _n, _w in CONST.items():
    C_AT[_n] = sum(CONST[m] for m in list(CONST)[:list(CONST).index(_n)])
N_CONST = sum(CONST.values())


def shape_constants():
    a = np.arange(P)
    c = {}
    c["ident"] = np.eye(P)
    c["ones"] = np.ones((P, P))
    low = np.where(a[None, :] <= a[:, None], 0.0, MASKED)
    zero = np.zeros((P, P))
    c["m_ij"] = np.concatenate([low, zero, low], 1)
    c["m_ji"] = np.concatenate([low.T, zero, low.T], 1)
    c["bd"] = ((a[:, None] // HGC == a[None, :] // HGC) & (a[:, None] <= a[None, :])).astype(float)
    c["reset"] = np.tile((np.arange(S) % HGC != 0).astype(float), (P, 1))
    half = P // 4 // 2
    inv = np.float32(500000.0) ** (-np.arange(half, dtype=np.float32) * np.float32(2.0) / np.float32(2 * half))
    ang = np.arange(S, dtype=np.float32)[None, :] * inv[:, None].astype(np.float32)
    c["cos"] = np.concatenate([np.cos(ang), np.cos(ang), np.ones((P - 2 * half, S))], 0)
    c["sin"] = np.concatenate([np.sin(ang), np.sin(ang), np.zeros((P - 2 * half, S))], 0)
    rot = np.zeros((P, P))
    for d in range(half):
        rot[d + half, d] = -1.0
        rot[d, d + half] = 1.0
    c["rot"] = rot
    sel = np.zeros((P, H, P))
    for h in range(H):
        sel[h, h, :] = 1.0
    c["sel"] = sel.reshape(P, H * P)
    return np.ascontiguousarray(np.concatenate([c[n] for n in CONST], 1).astype(np.float32))


def build(nc, x, ffn_norm, ffn_w_in, ffn_w_out, mix_norm, ab_w_in, ab_w_out, hgrn_lb_logits, hgrn_out_norm,
          conv_w, conv_b, cd_w_in, cd_w_out, mlstm_gate_bias, mlstm_out_norm, final_norm, consts, out):
    ctx = ExitStack()
    with ctx:
        def sb(name, shape, dt=F32):
            return ctx.enter_context(nc.sbuf_tensor(name, shape, dt))

        def sem(name):
            return ctx.enter_context(nc.semaphore(name))

        raw = sb("raw", [P, RING, SLOT])
        w_hi = sb("w_hi", [P, RING, SLOT], F32R)
        w_lo = sb("w_lo", [P, RING, SLOT], F32R)
        xs = sb("xs", [P, T, D])
        xn = sb("xn", [P, T, D])
        act = sb("act", [P, KD, S])
        x_hi = sb("x_hi", [P, KD, S], F32R)
        x_lo = sb("x_lo", [P, KD, S], F32R)
        y_hi = sb("y_hi", [P, KD, S], F32R)
        y_lo = sb("y_lo", [P, KD, S], F32R)
        mix = sb("mix", [P, 15, H * S])
        cst = sb("cst", [P, N_CONST])
        prow = sb("prow", [P, P])
        pcol = sb("pcol", [P, N_ROWS])
        fgain = sb("fgain", [P, D])
        gbias = sb("gbias", [H, 2])
        wgate = sb("wgate", [P, KD, 36])
        zb = sb("zb", [P, 512], BF16)
        col = sb("col", [P, 64])

        ch = ctx.enter_context(nc.psum_tensor("ch", [P, 4, 512], F32))
        acc = ctx.enter_context(nc.psum_tensor("acc", [P, 4, 512], F32))

        def const(name):
            return cst[:, C_AT[name]:C_AT[name] + CONST[name]]

        ident, ones = const("ident"), const("ones")
        eps_c, one_c = col[:, 0:1], col[:, 1:2]
        ssq, lnv, rstd = col[:, 2:4], col[:, 4:6], col[:, 6:8]
        lb, oml = col[:, 8:12], col[:, 12:16]
        lbt, lbe = col[:, 16:20], col[:, 20:32]
        gcol = col[:, 32:40]
        nmax, rsum = col[:, 40:48], col[:, 48:56]

        def gain(at):
            return pcol[:, at:at + 1]

        def m4(n):
            return mix[:, n, :].rearrange("p (h s) -> p h s", h=H)

        f_exp, f_sig = mix[:, 0, 0:2 * S].rearrange("p (j s) -> p j s", j=2), mix[:, 1, 0:2 * S].rearrange("p (j s) -> p j s", j=2)
        b_f, b_lf, b_b, b_eb, b_kc, b_kd, b_qe, b_q = (m4(n) for n in range(8))
        b_kt = mix[:, 0, :].rearrange("p (h t d) -> p h t d", h=H, t=T)
        b_at = mix[:, 1, :].rearrange("p (h t d) -> p h t d", h=H, t=T)
        b_v = mix[:, 8, :].rearrange("p (t c) -> p t c", t=T)
        b_s = mix[:, 9:13, :].rearrange("p n c -> p (n c)")[:, 0:7 * G].rearrange("p (c h v) -> p c h v", c=7, h=H)
        b_g, b_ge = m4(13), m4(6)
        b_c, b_z = m4(14), mix[:, 2:4, :].rearrange("p n c -> p (n c)")[:, 0:H * (S + 2)].rearrange("p (h s) -> p h s", h=H)
        b_o, b_sq = xn[:, 0, :].rearrange("p (h s) -> p h s", h=H), xn[:, 1, :].rearrange("p (h s) -> p h s", h=H)
        b_u, b_bg, b_rs = m4(5), m4(4), m4(7)
        c_q, c_k, c_lk, c_lq = m4(0), m4(1), m4(3), m4(4)
        c_v = mix[:, 2, :].rearrange("p (t c) -> p t c", t=T)
        c_lv = mix[:, 5, :].rearrange("p (t c) -> p t c", t=T)
        c_dt = mix[:, 6:8, :].rearrange("p n c -> p (n c)")[:, 0:H * 384].rearrange("p (h c) -> p h c", h=H)
        c_em = m4(8)
        c_p = mix[:, 9:11, :].rearrange("p n c -> p (n c)")[:, 0:H * 384].rearrange("p (h c) -> p h c", h=H)
        c_rs = mix[:, 9:11, :]
        c_pt = mix[:, 11:13, :].rearrange("p n c -> p (n c)")[:, 0:H * 384].rearrange("p (h c) -> p h c", h=H)
        c_oe, c_h, c_sq = m4(13), m4(14), m4(9)
        c_rn = m4(0)
        row = mix[0:H, 11:13, :].rearrange("p n c -> p (n c)").rearrange("p (n s) -> p n s", s=S)

        slot_in = [sem(f"slot_in{r}") for r in range(RING)]
        hi_done = sem("hi_done")
        lo_done = sem("lo_done")
        out_used = sem("out_used")
        small_in, x_in, const_in, fg_in = sem("small_in"), sem("x_in"), sem("const_in"), sem("fg_in")
        setup = sem("setup")
        prow_t, pcol_done = sem("prow_t"), sem("pcol_done")
        lb_sub, lb_exp = sem("lb_sub"), sem("lb_exp")
        dve, actq = sem("dve_order"), sem("act_order")
        x_ready = sem("x_ready")
        rstd_ready = sem("rstd_ready")
        xn_ready = sem("xn_ready")
        tp_ready = sem("tp_ready")
        xt_ready, xh_ready, xl_ready = sem("xt_ready"), sem("xh_ready"), sem("xl_ready")
        gate_ready, up_ready, gate_exp = sem("gate_ready"), sem("up_ready"), sem("gate_exp")
        hid, hid_hi, hid_lo = sem("hid"), sem("hid_hi"), sem("hid_lo")
        acc_done = sem("acc_done")
        chunk, chunk_out = sem("chunk"), sem("chunk_out")
        y_f, y_h, y_l = sem("y_f"), sem("y_h"), sem("y_l")
        f_ready, lf_ready, b_ready, e_ready, kd_ready, q_ready = (sem(n) for n in ("f_ready", "lf_ready", "b_ready", "e_ready", "kd_ready", "q_ready"))
        hg_at, hg_ev, hg_ds, hg_s, hg_o, hg_oc, hg_ss, hg_rs = (sem(n) for n in ("hg_at", "hg_ev", "hg_ds", "hg_s", "hg_o", "hg_oc", "hg_ss", "hg_rs"))
        gt_mm, gt_na, gt_ln, gt_rows, gt_tp, gt_col, gt_bc, gt_pre, gt_dt = (sem(n) for n in ("gt_mm", "gt_na", "gt_ln", "gt_rows", "gt_tp", "gt_col", "gt_bc", "gt_pre", "gt_dt"))
        mb_rot, mb_qk, mb_s, mb_sm, mb_p, mb_pn, mb_pt, mb_ptc, mb_o = (sem(n) for n in ("mb_rot", "mb_qk", "mb_s", "mb_sm", "mb_p", "mb_pn", "mb_pt", "mb_ptc", "mb_o"))
        ml_s, ml_w, ml_n, ml_h, ml_sq, ml_ss, ml_rs = (sem(n) for n in ("ml_s", "ml_w", "ml_n", "ml_h", "ml_sq", "ml_ss", "ml_rs"))
        out_done = sem("out_done")

        def slot3(t, r):
            return t[:, r, :].rearrange("p (k n) -> p k n", k=KD)

        def slot2(t, r):
            return t[:, r, :].rearrange("p (r n) -> p r n", r=2)

        AB_COLS = [(1, 0), (1, 1), (0, 0), (0, 1), (2, 0), (2, 1), (3, 0), (3, 1), (5, 0), (5, 1), (6, 0), (6, 1), (4, 0), (4, 1)]
        CD_COLS = [(4, 0), (4, 1), (5, 0), (5, 1), (6, 0), (6, 1), (1, 0), (1, 1), (0, 0), (0, 1), (2, 0), (2, 1), (3, 0), (3, 1)]
        AB_ROWS, CD_ROWS = [0, 2, 4, 6], [4, 6, 0, 2]
        TOK = (4, 5), (4, 5, 10, 11)

        block = ctx.enter_context(nc.Block())

        @block.sync
        def _(sp):
            def load(pos, n, dst, src, first=False):
                if not first:
                    sp.wait_ge(lo_done, n - (RING - 1))
                sp.dma_start(dst, src).then_inc(slot_in[pos], 16)

            def ffn(f, at):
                win, wout = ffn_w_in[f // 2, f % 2], ffn_w_out[f // 2, f % 2]

                def step(i, first=False):
                    n = FFN_BASE[f] + 3 * i
                    for kind in range(2):
                        load(kind, n + kind, slot3(raw, kind),
                             win[:, bass.ds(kind * F + i * PAIR, PAIR)].rearrange("(k p) n -> p k n", p=P), first)
                    load(2, n + 2, slot2(raw, 2),
                         wout[bass.ds(i * PAIR, PAIR), :].rearrange("(r p) n -> p r n", p=P), first)

                if f == 0:
                    step(0, True)
                with sp.Fori(1 if f == 0 else 0, ITER) as i:
                    step(i)

            def mixer(m):
                win, wout = (ab_w_in, cd_w_in)[m][0], (ab_w_out, cd_w_out)[m][0]
                for s in range(14):
                    g, half = (AB_COLS, CD_COLS)[m][s]
                    c0 = g * G + half * PAIR + (2 * H if m == 1 and g >= 4 else 0)
                    n = MIX_BASE[m] + s
                    load(n % RING, n, slot3(raw, n % RING), win[:, c0:c0 + PAIR].rearrange("(k p) n -> p k n", p=P))
                for s in range(4):
                    r0 = (AB_ROWS, CD_ROWS)[m][s] * P
                    n = MIX_BASE[m] + 14 + s
                    load(n % RING, n, slot2(raw, n % RING), wout[r0:r0 + PAIR, :].rearrange("(r p) n -> p r n", p=P))

            for kind, f in PHASES:
                if kind == "ffn":
                    ffn(f, f)
                else:
                    mixer(f)
            for t in range(T):
                sp.wait_ge(x_ready, 2 * 7 + t + 1)
                sp.dma_start(out[0, t * P:(t + 1) * P, :], xn[:, t, :]).then_inc(out_done, 16)
            sp.wait_ge(out_done, 16 * T)

        @block.gpsimd
        def _(pool):
            pool.memset(zb[:, :], 0.0).then_inc(setup, 1)
            pool.memset(eps_c, EPS).then_inc(setup, 1)
            pool.memset(one_c, 1.0).then_inc(setup, 1)
            pool.memset(wgate[:, :, :], 0.0).then_inc(setup, 1)
            pool.dma_start(fgain[:, :], final_norm.rearrange("(a n) -> a n", a=1).broadcast_to([P, D])).then_inc(fg_in, 16)
            pool.wait_ge(setup, 4)
            with nc.allow_non_contiguous_dma(reason="eight columns of gate weights, eight biases"):
                for j in range(2):
                    pool.dma_start(wgate[:, :, 32 * j:32 * j + H],
                                   cd_w_in[0][:, 4 * G + H * j:4 * G + H * j + H].rearrange("(k p) n -> p k n", p=P)).then_inc(fg_in, 16)
                pool.dma_start(gbias[:, :], mlstm_gate_bias[0].rearrange("j h -> h j")).then_inc(fg_in, 16)

        @block.scalar
        def _(ae):
            def loads():
                ae.dma_start(xs[:, :, :], x[0].rearrange("(t p) d -> p t d", p=P)).then_inc(x_in, 16)
                ae.dma_start(cst[:, :], consts).then_inc(const_in, 16)
                for at, src in ((C_FFN, ffn_norm.rearrange("l j (k p) -> (l j k) p", p=P)),
                                (C_MIX, mix_norm.rearrange("l (k p) -> (l k) p", p=P)),
                                (C_HGN, hgrn_out_norm[0]),
                                (C_CW, conv_w[0].rearrange("w (h p) -> (w h) p", p=P)),
                                (C_CB, conv_b[0].rearrange("(h p) -> h p", p=P)),
                                (C_MLN, mlstm_out_norm[0]),
                                (C_LB, hgrn_lb_logits.rearrange("r (h p) -> (r h) p", p=P))):
                    ae.dma_start(prow[at:at + src.shape[0], :], src).then_inc(small_in, 16)

            order = [0]

            def own(ins):
                order[0] += 1
                ins.then_inc(actq, 1)
                ae.wait_ge(actq, order[0])

            def round_slot(pos, landed):
                ae.wait_ge(slot_in[pos], landed)
                ae.activation(w_hi[:, pos, :], raw[:, pos, :], ACT.Copy).then_inc(hi_done, 1)

            def split_out(f, i):
                n = FFN_BASE[f] + 2
                ae.wait_ge(out_used, OUT_FFN[f] + i)
                round_slot(n % RING, 16 * (n // RING + 1) + 16 * i)

            def split_in(f, i, kind):
                n = FFN_BASE[f] + RING + kind
                ae.wait_ge((gate_ready, up_ready)[kind], 2 * ITER * f + 2 * i + 2)
                round_slot(n % RING, 16 * (n // RING + 1) + 16 * i)

            def norm(m):
                for t in range(T):
                    ae.wait_ge(x_ready, 2 * m + t + 1)
                    own(ae.activation(xn[:, t, :], xs[:, t, :], ACT.Square, accum_out=ssq[:, t:t + 1]))
                    own(ae.activation(lnv[:, t:t + 1], ssq[:, t:t + 1], ACT.Ln, bias=eps_c, scale=1.0 / D))
                    ae.activation(rstd[:, t:t + 1], lnv[:, t:t + 1], ACT.Exp, scale=-0.5).then_inc(rstd_ready, 1)
                if m == 6:
                    return
                for b in range(4):
                    t, half = b // 2, b % 2
                    sl = (slice(None), slice(4 * half, 4 * half + 4), slice(t * P, (t + 1) * P))
                    ae.wait_ge(xt_ready, 4 * m + b + 1)
                    ae.activation(x_hi[sl], act[sl], ACT.Copy).then_inc(xh_ready, 1)

            def ffn(f):
                def step(i, last=False, f_first=False):
                    q0 = 2 * ITER * f + 2 * i

                    def hidden(j):
                        ae.wait_ge(hid, q0 + j + 1)
                        ae.activation(y_hi[:, j, :], act[:, j, :], ACT.Copy).then_inc(hid_hi, 1)

                    if not f_first:
                        split_out(f, i)
                    for j in range(2):
                        ae.wait_ge(gate_ready, q0 + j + 1)
                        ae.activation(f_exp[:, j, :], ch[:, 2 * j, 0:S], ACT.Exp, scale=-1.0).then_inc(gate_exp, 1)
                        if j == 0:
                            hidden(0)
                    if not last:
                        split_in(f, i, 0)
                    hidden(1)
                    if not last:
                        split_in(f, i, 1)

                if f == 0:
                    step(0, f_first=True)
                with ae.Fori(1 if f == 0 else 0, ITER - 1 if f == 3 else ITER) as i:
                    step(i)
                if f == 3:
                    step(ITER - 1, last=True)

            def after(m, s):
                if s < 0:
                    ae.wait_ge(out_used, OUT_MIX[m])
                elif s < 14:
                    ae.wait_ge(chunk, CHUNKS * m + 2 * s + 2)
                else:
                    ae.wait_ge(out_used, OUT_MIX[m] + s - 13)
                n = MIX_BASE[m] + s + RING
                round_slot(n % RING, 16 * (n // RING + 1))

            def chunks(m, s, *moves):
                for j in range(2):
                    c = 2 * s + j
                    ae.wait_ge(chunk, CHUNKS * m + c + 1)
                    src = ch[:, c % 4, 0:S]
                    for k, (dst, func, scale) in enumerate(moves):
                        ins = ae.activation(dst(j), src, func, scale=scale)
                    ins.then_inc(chunk_out, 1)
                after(m, s)

            def y_split(m, parts):
                for k0, k1, count in parts:
                    ae.wait_ge(y_f, count)
                    ae.activation(y_hi[:, k0:k1, :], act[:, k0:k1, :], ACT.Copy).then_inc(y_h, 1)

            def mixer_ab():
                after(0, -1)
                for s in (0, 1):
                    chunks(0, s, (lambda j: b_f[:, 2 * s + j, :], ACT.Exp, -1.0))
                for p in range(2):
                    ae.wait_ge(f_ready, p + 1)
                    ae.activation(b_lf[:, 2 * p:2 * p + 2, :], b_f[:, 2 * p:2 * p + 2, :], ACT.Ln).then_inc(lf_ready, 1)
                for s in (2, 3):
                    chunks(0, s, (lambda j: b_qe[:, 2 * s - 4 + j, :], ACT.Exp, -1.0), (lambda j: b_q[:, 2 * s - 4 + j, :], ACT.Copy, 1.0))
                    if s == 2:
                        for p in range(2):
                            h = slice(2 * p, 2 * p + 2)
                            ae.wait_ge(b_ready, p + 1)
                            ae.activation(b_eb[:, h, :], b_b[:, h, :], ACT.Exp).then_inc(actq, 1)
                            ae.activation(b_lf[:, h, :], b_lf[:, h, :], ACT.Exp)
                            order[0] += 1
                            ae.wait_ge(actq, order[0])
                            ae.activation(b_b[:, h, :], b_b[:, h, :], ACT.Exp, scale=-1.0).then_inc(e_ready, 1)
                for s in (4, 5):
                    chunks(0, s, (lambda j: b_v[:, j, (s - 4) * PAIR:(s - 3) * PAIR], ACT.Copy, 1.0))
                for s in (6, 7):
                    if s == 6:
                        ae.wait_ge(q_ready, 2)
                    chunks(0, s, (lambda j: b_ge[:, 2 * s - 12 + j, :], ACT.Exp, -1.0), (lambda j: b_g[:, 2 * s - 12 + j, :], ACT.Copy, 1.0))
                chunks(0, 8, (lambda j: b_c[:, j, :], ACT.Copy, 1.0))
                for h in range(H):
                    ae.wait_ge(hg_o, h + 1)
                    ae.activation(b_o[:, h, :], acc[:, h, 0:S], ACT.Copy)
                    ae.activation(b_sq[:, h, :], acc[:, h, 0:S], ACT.Square).then_inc(hg_oc, 1)
                chunks(0, 9, (lambda j: b_c[:, 2 + j, :], ACT.Copy, 1.0))
                for h in range(H):
                    ae.wait_ge(hg_ss, h + 1)
                    own(ae.activation(b_rs[:, h, :], acc[:, h, 0:S], ACT.Ln, bias=eps_c, scale=1.0 / P))
                    ae.activation(b_rs[:, h, :], b_rs[:, h, :], ACT.Exp, scale=-0.5).then_inc(hg_rs, 1)
                for s in (10, 11):
                    chunks(0, s, (lambda j: b_u[:, 2 * s - 20 + j, :], ACT.Copy, 1.0))
                    if s == 10:
                        y_split(0, [(0, 4, 1)])
                for s in (12, 13):
                    chunks(0, s, (lambda j: b_bg[:, 2 * s - 24 + j, :], ACT.Copy, 1.0))
                    y_split(0, [(2 * s - 20, 2 * s - 18, s - 10)])
                for s in (14, 15, 16):
                    after(0, s)

            def mixer_cd():
                after(1, -1)
                for s in (0, 1):
                    chunks(1, s, (lambda j: c_q[:, 2 * s + j, :], ACT.Copy, 1.0))
                ae.wait_ge(gt_na, 1)
                own(ae.activation(row[:, 2, :], row[:, 2, :], ACT.Exp))
                ae.activation(row[:, 3, :], row[:, 2, :], ACT.Ln, bias=one_c[0:H, :]).then_inc(gt_ln, 1)
                for s in (2, 3):
                    chunks(1, s, (lambda j: c_k[:, 2 * s - 4 + j, :], ACT.Copy, 1.0))
                for h in range(H):
                    ae.wait_ge(gt_pre, h + 1)
                    ae.activation(c_em[:, h, :], acc[:, h, S:2 * S], ACT.Exp)
                    ae.activation(c_dt[:, h, 0:S], c_dt[:, h, 0:S], ACT.Exp, bias=gcol[:, h:h + 1])
                    ae.activation(c_dt[:, h, S:384], c_dt[:, h, S:384], ACT.Exp, bias=gcol[:, H + h:H + h + 1]).then_inc(gt_dt, 1)
                for s in (4, 5):
                    chunks(1, s, (lambda j: c_v[:, j, (s - 4) * PAIR:(s - 3) * PAIR], ACT.Copy, 1.0))
                chunks(1, 6, (lambda j: c_lk[:, j, :], ACT.Copy, 1.0))
                for h in range(H):
                    ae.wait_ge(mb_sm, h + 1)
                    ae.activation(c_p[:, h, 0:P], c_p[:, h, 0:P], ACT.Exp, bias=nmax[:, 2 * h:2 * h + 1],
                                  scale=P ** -0.5, accum_out=rsum[:, 2 * h:2 * h + 1])
                    ae.activation(c_p[:, h, P:384], c_p[:, h, P:384], ACT.Exp, bias=nmax[:, 2 * h + 1:2 * h + 2],
                                  scale=P ** -0.5, accum_out=rsum[:, 2 * h + 1:2 * h + 2]).then_inc(mb_p, 1)
                chunks(1, 7, (lambda j: c_lk[:, 2 + j, :], ACT.Copy, 1.0))
                for h in range(H):
                    ae.wait_ge(mb_pt, h + 1)
                    ae.activation(c_pt[:, h, :], acc[:, h, 0:384], ACT.Copy).then_inc(mb_ptc, 1)
                chunks(1, 8, (lambda j: c_lq[:, j, :], ACT.Copy, P ** -0.5))
                for h in range(H):
                    ae.wait_ge(mb_o, h + 1)
                    ins = ae.activation(act[:, 4 + h, :], acc[:, h, 0:S], ACT.Copy)
                    ins.then_inc(y_f, 1)
                chunks(1, 9, (lambda j: c_lq[:, 2 + j, :], ACT.Copy, P ** -0.5))
                y_split(1, [(4, 8, 3 + H)])
                for s in (10, 11):
                    chunks(1, s, (lambda j: c_lv[:, j, (s - 10) * PAIR:(s - 9) * PAIR], ACT.Copy, 1.0))
                for s in (12, 13):
                    chunks(1, s, (lambda j: c_oe[:, 2 * s - 24 + j, :], ACT.Exp, -1.0))
                    if s == 12:
                        for h in range(H):
                            ae.wait_ge(ml_h, h + 1)
                            ae.activation(c_sq[:, h, :], c_h[:, h, :], ACT.Square).then_inc(ml_sq, 1)
                after(1, 14)
                for h in range(H):
                    ae.wait_ge(ml_ss, h + 1)
                    own(ae.activation(c_rn[:, h, :], ch[:, h, 0:S], ACT.Ln, bias=eps_c, scale=1.0 / P))
                    ae.activation(c_rn[:, h, :], c_rn[:, h, :], ACT.Exp, scale=-0.5).then_inc(ml_rs, 1)
                y_split(1, [(0, 2, 3 + H + 1), (2, 4, 3 + H + 2)])
                for s in (15, 16):
                    after(1, s)

            loads()
            ae.wait_ge(setup, 3)
            for n in range(RING):
                round_slot(n, 16)
            ae.wait_ge(lb_sub, 1)
            ae.activation(lbe, lbe, ACT.Exp).then_inc(lb_exp, 1)
            m = 0
            for kind, f in PHASES:
                norm(m)
                m += 1
                if kind == "ffn":
                    ffn(f)
                elif kind == "ab":
                    mixer_ab()
                else:
                    mixer_cd()
            norm(6)

        @block.vector
        def _(v):
            order = [0, 0]

            def own(ins):
                order[0] += 1
                ins.then_inc(dve, 1)
                v.wait_ge(dve, order[0] + order[1])

            def rest(n, pos, wait_used=True):
                v.wait_ge(hi_done, n + 1)
                v.tensor_tensor(w_lo[:, pos, :], raw[:, pos, :], w_hi[:, pos, :].bitcast(F32), ALU.subtract).then_inc(lo_done, 1)

            def residual(m, scale):
                for t in range(T):
                    if t == 0:
                        v.wait_ge(acc_done, m)
                    for half in range(2):
                        dst = xs[:, t, 512 * half:512 * half + 512]
                        ins = v.scalar_tensor_tensor(out=dst, in0=acc[:, 2 * t + half, :], scalar=scale, in1=dst, op0=ALU.mult, op1=ALU.add)
                    ins.then_inc(x_ready, 1)

            def norm(m, gains):
                for t in range(T):
                    v.wait_ge(rstd_ready, 2 * m + t + 1)
                    v.wait_ge(x_ready, 2 * m + t + 1)
                    v.tensor_scalar(xn[:, t, :], xs[:, t, :], rstd[:, t:t + 1], None, ALU.mult).then_inc(xn_ready, 1)

                def low(b):
                    t, half = b // 2, b % 2
                    sl = (slice(None), slice(4 * half, 4 * half + 4), slice(t * P, (t + 1) * P))
                    v.wait_ge(xh_ready, 4 * m + b + 1)
                    v.tensor_tensor(x_lo[sl], act[sl], x_hi[sl].bitcast(F32), ALU.subtract).then_inc(xl_ready, 1)

                for b in range(4):
                    t, half = b // 2, b % 2
                    v.wait_ge(tp_ready, 4 * m + b + 1)
                    g = pcol[:, gains + 4 * half:gains + 4 * half + 4].unsqueeze(2).broadcast_to([P, 4, P])
                    v.tensor_tensor(act[:, 4 * half:4 * half + 4, t * P:(t + 1) * P],
                                    ch[:, b, :].rearrange("p (k s) -> p k s", k=4), g, ALU.mult).then_inc(xt_ready, 1)
                    if b:
                        low(b - 1)
                low(3)

            def ffn(f):
                def step(i, last=False, f_first=False):
                    q0 = 2 * ITER * f + 2 * i
                    n0 = FFN_BASE[f] + 3 * i

                    def silu(j):
                        v.wait_ge(gate_exp, q0 + j + 1)
                        own(v.tensor_scalar(f_sig[:, j, :], f_exp[:, j, :], 1.0, None, ALU.add))
                        own(v.reciprocal(f_sig[:, j, :], f_sig[:, j, :]))
                        own(v.tensor_tensor(f_sig[:, j, :], ch[:, 2 * j, 0:S], f_sig[:, j, :], ALU.mult))

                    def hidden(j):
                        v.wait_ge(up_ready, q0 + j + 1)
                        v.tensor_tensor(act[:, j, :], ch[:, 2 * j + 1, 0:S], f_sig[:, j, :], ALU.mult).then_inc(hid, 1)
                        v.wait_ge(hid_hi, q0 + j + 1)
                        v.tensor_tensor(y_lo[:, j, :], act[:, j, :], y_hi[:, j, :].bitcast(F32), ALU.subtract).then_inc(hid_lo, 1)

                    if not f_first:
                        rest(n0 + 2, 2)
                    silu(0)
                    hidden(0)
                    silu(1)
                    if not last:
                        rest(n0 + 3, 0)
                    hidden(1)
                    if not last:
                        rest(n0 + 4, 1)

                STEPS = 6
                first = 0
                if f == 0:
                    step(0, f_first=True)
                    first = 1
                base = order[0]
                end = ITER - 1 if f == 3 else ITER
                with v.Fori(first, end) as i:
                    order[0], order[1] = base, (i - first) * STEPS
                    step(i)
                order[0], order[1] = base + (end - first) * STEPS, 0
                if f == 3:
                    step(ITER - 1, last=True)

            def after(m, s):
                n = MIX_BASE[m] + s + RING
                rest(n, n % RING)

            def sigmoid(buf):
                own(v.tensor_scalar(buf, buf, 1.0, None, ALU.add))
                own(v.reciprocal(buf, buf))

            def y_rest(parts):
                for k0, k1, count in parts:
                    v.wait_ge(y_h, count)
                    v.tensor_tensor(y_lo[:, k0:k1, :], act[:, k0:k1, :], y_hi[:, k0:k1, :].bitcast(F32), ALU.subtract).then_inc(y_l, 1)

            def mixer_ab():
                def forget(p):
                    h = slice(2 * p, 2 * p + 2)
                    v.wait_ge(chunk_out, 2 * p + 2)
                    sigmoid(b_f[:, h, :])
                    for a in (2 * p, 2 * p + 1):
                        v.tensor_scalar(b_f[:, a, :], b_f[:, a, :], oml[:, a:a + 1], lb[:, a:a + 1], ALU.mult, ALU.add).then_inc(dve, 1)
                    order[0] += 2
                    v.wait_ge(dve, order[0])
                    v.tensor_scalar(b_kc[:, h, :], b_f[:, h, :], -1.0, 1.0, ALU.mult, ALU.add).then_inc(f_ready, 1)

                def cumulate(p):
                    h = slice(2 * p, 2 * p + 2)
                    v.wait_ge(lf_ready, p + 1)
                    for a in (2 * p, 2 * p + 1):
                        ins = v.tensor_tensor_scan(b_b[:, a, :], const("reset"), b_lf[:, a, :], 0.0, ALU.mult, ALU.add)
                        ins.then_inc(dve, 1)
                    order[0] += 2
                    v.wait_ge(dve, order[0])
                    for a in (2 * p, 2 * p + 1):
                        bb = b_b[:, a, :].rearrange("p (c s) -> p c s", s=HGC)
                        ins = v.tensor_tensor(b_lf[:, a, :].rearrange("p (c s) -> p c s", s=HGC),
                                              bb[:, :, HGC - 1:HGC].broadcast_to([P, S // HGC, HGC]), bb, ALU.subtract)
                    ins.then_inc(b_ready, 1)

                def keys(p):
                    h = slice(2 * p, 2 * p + 2)
                    v.wait_ge(e_ready, p + 1)
                    own(v.tensor_tensor(b_kd[:, h, :], b_kc[:, h, :], b_b[:, h, :], ALU.mult))
                    v.tensor_tensor(b_kc[:, h, :], b_kc[:, h, :], b_lf[:, h, :], ALU.mult).then_inc(kd_ready, 1)

                def queries(p):
                    h = slice(2 * p, 2 * p + 2)
                    v.wait_ge(chunk_out, 8 - 2 + 2 * p)
                    sigmoid(b_qe[:, h, :])
                    own(v.tensor_tensor(b_q[:, h, :], b_q[:, h, :], b_qe[:, h, :], ALU.mult))
                    v.tensor_tensor(b_q[:, h, :], b_q[:, h, :], b_eb[:, h, :], ALU.mult).then_inc(q_ready, 1)

                def states(t):
                    v.wait_ge(hg_ds, t + 1)
                    for c in range(4 * t, min(4 * t + 4, 7)):
                        for h in range(H):
                            src = acc[:, c % 4, h * P:(h + 1) * P]
                            if c == 0:
                                ins = v.tensor_copy(b_s[:, 0, h, :], src)
                            else:
                                ins = v.scalar_tensor_tensor(out=b_s[:, c, h, :], in0=b_s[:, c - 1, h, :],
                                                             scalar=b_eb[:, h, c * HGC + HGC - 1:c * HGC + HGC], in1=src, op0=ALU.mult, op1=ALU.add)
                            ins.then_inc(dve, 1)
                        order[0] += H
                        v.wait_ge(dve, order[0])
                    v.sem_inc(hg_s, 1)

                after(0, -1)
                forget(0)
                after(0, 0)
                forget(1)
                after(0, 1)
                cumulate(0)
                cumulate(1)
                after(0, 2)
                keys(0)
                keys(1)
                queries(0)
                after(0, 3)
                queries(1)
                after(0, 4)
                for h in range(H):
                    v.wait_ge(hg_at, h + 1)
                    v.tensor_copy(b_kt[:, h, :, :], acc[:, h, 0:S].rearrange("p (t d) -> p t d", t=T))
                    v.tensor_tensor(b_at[:, h, :, :], acc[:, h, S:2 * S].rearrange("p (t d) -> p t d", t=T),
                                    const("bd").unsqueeze(1).broadcast_to([P, T, P]), ALU.mult).then_inc(hg_ev, 1)
                after(0, 5)
                after(0, 6)
                states(0)
                after(0, 7)
                states(1)
                after(0, 8)
                v.wait_ge(chunk_out, 16)
                sigmoid(b_ge[:, :, :])
                v.tensor_tensor(b_g[:, :, :], b_g[:, :, :], b_ge[:, :, :], ALU.mult).then_inc(dve, 1)
                order[0] += 1
                after(0, 9)
                for h in range(H):
                    v.wait_ge(hg_rs, h + 1)
                    own(v.scalar_tensor_tensor(out=b_o[:, h, :], in0=b_o[:, h, :], scalar=gain(C_HGN + h), in1=b_rs[:, h, :], op0=ALU.mult, op1=ALU.mult))
                    v.tensor_tensor(act[:, h, :], b_o[:, h, :], b_g[:, h, :], ALU.mult).then_inc(dve, 1)
                    order[0] += 1
                v.wait_ge(dve, order[0])
                v.sem_inc(y_f, 1)
                own(v.memset(b_z[:, :, 0:2], 0.0))
                for p in range(2):
                    after(0, 10 + p)
                    h = slice(2 * p, 2 * p + 2)
                    v.wait_ge(chunk_out, 22 + 2 * p)
                    own(v.tensor_tensor(b_z[:, h, 2:S + 2], b_c[:, h, :], b_u[:, h, :], ALU.mult))
                    if p == 0:
                        y_rest([(0, 4, 1)])
                for h in range(H):
                    own(v.tensor_scalar(b_c[:, h, :], b_z[:, h, 2:S + 2], gain(C_CW + 2 * H + h), gain(C_CB + h), ALU.mult, ALU.add))
                    for w in (1, 0):
                        own(v.scalar_tensor_tensor(out=b_c[:, h, :], in0=b_z[:, h, w:S + w], scalar=gain(C_CW + w * H + h), in1=b_c[:, h, :], op0=ALU.mult, op1=ALU.add))
                for p in range(2):
                    h = slice(2 * p, 2 * p + 2)
                    v.wait_ge(chunk_out, 26 + 2 * p)
                    v.tensor_tensor(act[:, 4 + 2 * p:6 + 2 * p, :], b_c[:, h, :], b_bg[:, h, :], ALU.mult).then_inc(y_f, 1)
                    y_rest([(4 + 2 * p, 6 + 2 * p, 2 + p)])
                    after(0, 12 + p)
                for s in (14, 15, 16):
                    after(0, s)

            def mixer_cd():
                after(1, -1)
                v.wait_ge(gt_mm, 1)
                v.wait_ge(fg_in, 64)
                v.tensor_scalar(row[:, 0, :], acc[0:H, 0, 0:S], gbias[:, 0:1], None, ALU.add)
                own(v.tensor_scalar(row[:, 1, :], acc[32:32 + H, 0, 0:S], gbias[:, 1:2], None, ALU.add))
                v.scalar_tensor_tensor(out=row[:, 2, :], in0=row[:, 1, :], scalar=-1.0, in1=row[:, 1, :], op0=ALU.mult, op1=ALU.min).then_inc(gt_na, 1)
                after(1, 0)
                v.wait_ge(gt_ln, 1)
                own(v.scalar_tensor_tensor(out=row[:, 1, :], in0=row[:, 1, :], scalar=0.0, in1=row[:, 3, :], op0=ALU.min, op1=ALU.subtract))
                one_row = const("ones")[0:H, 0:1].broadcast_to([H, S])
                own(v.tensor_tensor_scan(row[:, 4, :], one_row, row[:, 1, :], 0.0, ALU.mult, ALU.add))
                own(v.tensor_tensor(row[:, 5, :], row[:, 0, :], row[:, 4, :], ALU.subtract))
                own(v.tensor_tensor_scan(row[:, 2, :], one_row, row[:, 5, :], 0.0, ALU.mult, ALU.max))
                own(v.tensor_scalar(row[:, 6, :], row[:, 2, :], -1.0, None, ALU.mult))
                v.tensor_tensor(row[:, 7, :], row[:, 6, :], row[:, 4, :], ALU.subtract).then_inc(gt_rows, 1)
                after(1, 1)
                v.wait_ge(gt_tp, 1)
                v.tensor_copy(gcol, acc[:, 0, 0:2 * H]).then_inc(gt_col, 1)
                after(1, 2)
                for h in range(H):
                    v.wait_ge(gt_bc, h + 1)
                    v.tensor_tensor(c_dt[:, h, 0:S], acc[:, h, 0:S], const("m_ji")[:, 0:S], ALU.add)
                    v.tensor_tensor(c_dt[:, h, S:384], acc[:, h, P:S], const("m_ji")[:, S:384], ALU.add).then_inc(gt_pre, 1)
                after(1, 3)
                cos = const("cos").unsqueeze(1).broadcast_to([P, H, S])
                sin = const("sin").unsqueeze(1).broadcast_to([P, 2, S])
                v.wait_ge(chunk_out, CHUNKS + 8)
                for n, buf in enumerate((c_q, c_k)):
                    for half in range(2):
                        v.wait_ge(mb_rot, 2 * n + half + 1)
                        v.tensor_tensor(c_rs[:, n, 512 * half:512 * half + 512].rearrange("p (h s) -> p h s", h=2),
                                        acc[:, 2 * n + half, :].rearrange("p (h s) -> p h s", h=2), sin, ALU.mult).then_inc(dve, 1)
                    order[0] += 2
                    own(v.tensor_tensor(buf[:, :, :], buf[:, :, :], cos, ALU.mult))
                    v.tensor_tensor(buf[:, :, :], buf[:, :, :], c_rs[:, n, :].rearrange("p (h s) -> p h s", h=H), ALU.add).then_inc(mb_qk, 1)
                after(1, 4)
                after(1, 5)
                v.wait_ge(mb_qk, 2)
                for h in range(H):
                    v.wait_ge(mb_s, h + 1)
                    own(v.tensor_tensor(c_p[:, h, :], acc[:, h, 0:384], const("m_ij"), ALU.add))
                    v.tensor_reduce(nmax[:, 2 * h:2 * h + 1], c_p[:, h, 0:P], AX.X, ALU.max)
                    own(v.tensor_reduce(nmax[:, 2 * h + 1:2 * h + 2], c_p[:, h, P:384], AX.X, ALU.max))
                    v.tensor_scalar(nmax[:, 2 * h:2 * h + 2], nmax[:, 2 * h:2 * h + 2], -(P ** -0.5), None, ALU.mult).then_inc(mb_sm, 1)
                after(1, 6)
                for h in range(H):
                    v.wait_ge(mb_p, h + 1)
                    own(v.reciprocal(rsum[:, 2 * h:2 * h + 2], rsum[:, 2 * h:2 * h + 2]))
                    v.tensor_scalar(c_p[:, h, 0:P], c_p[:, h, 0:P], rsum[:, 2 * h:2 * h + 1], None, ALU.mult)
                    v.tensor_scalar(c_p[:, h, P:384], c_p[:, h, P:384], rsum[:, 2 * h + 1:2 * h + 2], None, ALU.mult).then_inc(mb_pn, 1)
                for s in (7, 8, 9):
                    after(1, s)
                y_rest([(4, 8, 4)])
                for h in range(H):
                    v.wait_ge(ml_s, h + 1)
                    v.wait_ge(gt_dt, h + 1)
                    v.tensor_tensor(c_dt[:, h, :], acc[:, h, 0:384], c_dt[:, h, :], ALU.mult).then_inc(ml_w, 1)
                for s in (10, 11):
                    after(1, s)
                for h in range(H):
                    v.wait_ge(ml_n, h + 1)
                    own(v.tensor_tensor(c_em[:, h, :], acc[:, h, S:2 * S], c_em[:, h, :], ALU.max))
                    own(v.scalar_tensor_tensor(out=c_em[:, h, :], in0=acc[:, h, S:2 * S], scalar=-1.0, in1=c_em[:, h, :], op0=ALU.mult, op1=ALU.max))
                    own(v.reciprocal(c_em[:, h, :], c_em[:, h, :]))
                    v.tensor_tensor(c_h[:, h, :], acc[:, h, 0:S], c_em[:, h, :], ALU.mult).then_inc(ml_h, 1)
                after(1, 12)
                v.wait_ge(chunk_out, 2 * CHUNKS)
                sigmoid(c_oe[:, :, :])
                after(1, 13)
                for h in range(H):
                    v.wait_ge(ml_rs, h + 1)
                    own(v.scalar_tensor_tensor(out=c_h[:, h, :], in0=c_h[:, h, :], scalar=gain(C_MLN + h), in1=c_rn[:, h, :], op0=ALU.mult, op1=ALU.mult))
                    ins = v.tensor_tensor(act[:, h, :], c_h[:, h, :], c_oe[:, h, :], ALU.mult)
                    if h % 2:
                        ins.then_inc(y_f, 1)
                y_rest([(0, 2, 5), (2, 4, 6)])
                for s in (14, 15, 16):
                    after(1, s)

            for n in range(RING):
                rest(n, n)
            v.wait_ge(prow_t, 1)
            v.tensor_copy(pcol[:, :], ch[:, 0, 0:N_ROWS]).then_inc(pcol_done, 1)
            v.wait_ge(pcol_done, 1)
            rows = pcol[:, C_LB:C_LB + 12].rearrange("p (r h) -> p r h", r=3)
            own(v.tensor_tensor(lbt, rows[:, 0, :], rows[:, 1, :], ALU.max))
            own(v.tensor_tensor(lbt, lbt, rows[:, 2, :], ALU.max))
            e = lbe.rearrange("p (r h) -> p r h", r=3)
            v.tensor_tensor(e, rows, lbt.unsqueeze(1).broadcast_to([P, 3, H]), ALU.subtract).then_inc(lb_sub, 1)
            v.wait_ge(lb_exp, 1)
            own(v.tensor_tensor(lbt, e[:, 0, :], e[:, 1, :], ALU.add))
            own(v.tensor_tensor(lbt, lbt, e[:, 2, :], ALU.add))
            own(v.reciprocal(lbt, lbt))
            own(v.tensor_tensor(lb, e[:, 0, :], lbt, ALU.mult))
            own(v.tensor_scalar(oml, lb, -1.0, 1.0, ALU.mult, ALU.add))
            v.wait_ge(x_in, 16)
            v.sem_inc(x_ready, 2)
            gains = [0, C_MIX, 8, 16, C_MIX + 8, 24]
            m = 0
            for kind, f in PHASES:
                norm(m, gains[m])
                m += 1
                if kind == "ffn":
                    ffn(f)
                elif kind == "ab":
                    mixer_ab()
                else:
                    mixer_cd()
                residual(m, 0.5 if kind == "ffn" else 1.0)
            v.wait_ge(fg_in, 64)
            for t in range(T):
                v.wait_ge(rstd_ready, 2 * 6 + t + 1)
                v.wait_ge(x_ready, 2 * 6 + t + 1)
                own(v.tensor_scalar(xn[:, t, :], xs[:, t, :], rstd[:, t:t + 1], None, ALU.mult))
                v.tensor_tensor(xn[:, t, :], xn[:, t, :], fgain[:, :], ALU.mult).then_inc(x_ready, 1)

        @block.tensor
        def _(pe):
            def three(dst, l_hi, l_lo, r_hi, r_lo, start, stop):
                pe.matmul(dst, l_hi, r_hi, start=start, stop=False, skip_group_check=True)
                pe.matmul(dst, l_hi, r_lo, start=False, stop=False, skip_group_check=True)
                return pe.matmul(dst, l_lo, r_hi, start=False, stop=stop, skip_group_check=True)

            def channels(dst, pos, j):
                c = slice(j * P, (j + 1) * P)
                for k in range(KD):
                    ins = three(dst, slot3(w_hi, pos)[:, k, c], slot3(w_lo, pos)[:, k, c], x_hi[:, k, :], x_lo[:, k, :], k == 0, k == KD - 1)
                return ins

            def tokens(dst, pos, t):
                c = slice(t * P, (t + 1) * P)
                for k in range(KD):
                    ins = three(dst, x_hi[:, k, c], x_lo[:, k, c], slot3(w_hi, pos)[:, k, :], slot3(w_lo, pos)[:, k, :], k == 0, k == KD - 1)
                return ins

            def project(pos, r, k, start, stop):
                for t in range(T):
                    c = slice(t * P, (t + 1) * P)
                    for half in range(2):
                        w = slice(512 * half, 512 * half + 512)
                        ins = three(acc[:, 2 * t + half, :], y_hi[:, k, c], y_lo[:, k, c], slot2(w_hi, pos)[:, r, w], slot2(w_lo, pos)[:, r, w], start, stop)
                return ins

            def norm(m):
                for t in range(T):
                    pe.wait_ge(xn_ready, 2 * m + t + 1)
                    for half in range(2):
                        for k in range(4):
                            ins = pe.transpose(ch[:, 2 * t + half, k * P:(k + 1) * P], xn[:, t, (4 * half + k) * P:(4 * half + k + 1) * P], ident)
                        ins.then_inc(tp_ready, 1)

            def ffn(f, m):
                def step(i):
                    q0 = 2 * ITER * f + 2 * i
                    n0 = FFN_BASE[f] + 3 * i
                    for j in range(2):
                        if j == 0:
                            pe.wait_ge(lo_done, n0 + 1)
                        channels(ch[:, 2 * j, 0:S], 0, j).then_inc(gate_ready, 1)
                        if j == 0:
                            pe.wait_ge(lo_done, n0 + 2)
                        channels(ch[:, 2 * j + 1, 0:S], 1, j).then_inc(up_ready, 1)
                    pe.wait_ge(lo_done, n0 + 3)
                    for j in range(2):
                        pe.wait_ge(hid_lo, q0 + j + 1)
                        ins = project(2, j, j, False, False)
                    ins.then_inc(out_used, 1)

                for b in range(4):
                    pe.matmul(acc[:, b, :], zb[:, 0:P], zb[:, :], start=True, stop=False, skip_group_check=True)
                with pe.Fori(0, ITER - 1) as i:
                    step(i)
                step(ITER - 1)
                ins = None
                for b in range(4):
                    ins = pe.matmul(acc[:, b, :], zb[:, 0:P], zb[:, :], start=False, stop=True, skip_group_check=True)
                ins.then_inc(acc_done, 1)

            def slot(m, s):
                n = MIX_BASE[m] + s
                pe.wait_ge(lo_done, n + 1)
                for j in range(2):
                    c = 2 * s + j
                    if c >= 4:
                        pe.wait_ge(chunk_out, CHUNKS * m + c - 3)
                    f = tokens if s in TOK[m] else channels
                    ins = f(ch[:, c % 4, 0:S], n % RING, j)
                    ins.then_inc(chunk, 1)

            def out_slot(m, s, y_count):
                n = MIX_BASE[m] + 14 + s
                pe.wait_ge(lo_done, n + 1)
                pe.wait_ge(y_l, y_count)
                k0 = (AB_ROWS, CD_ROWS)[m][s]
                for r in range(2):
                    ins = project(n % RING, r, k0 + r, s == 0 and r == 0, s == 3 and r == 1)
                ins.then_inc(out_used, 1)
                return ins

            def mixer_ab():
                for s in range(5):
                    slot(0, s)
                pe.wait_ge(kd_ready, 2)
                pe.wait_ge(q_ready, 2)
                for h in range(H):
                    for t in range(T):
                        pe.transpose(acc[:, h, t * P:(t + 1) * P], b_kc[:, h, t * P:(t + 1) * P], ident)
                    for t in range(T):
                        c = slice(t * P, (t + 1) * P)
                        ins = pe.matmul(acc[:, h, S + t * P:S + (t + 1) * P], b_kd[:, h, c], b_q[:, h, c], start=True, stop=True)
                    ins.then_inc(hg_at, 1)
                slot(0, 5)
                slot(0, 6)
                pe.wait_ge(hg_ev, H)
                pe.wait_ge(chunk_out, 12)
                for t in range(T):
                    if t:
                        slot(0, 7)
                        pe.wait_ge(hg_s, 1)
                    for c in range(4 if t == 0 else 3):
                        r = slice(HGC * c, HGC * (c + 1))
                        for h in range(H):
                            ins = pe.matmul(acc[:, c, h * P:(h + 1) * P], b_kt[r, h, t, :], b_v[r, t, h * P:(h + 1) * P], start=True, stop=True)
                    ins.then_inc(hg_ds, 1)
                slot(0, 8)
                pe.wait_ge(hg_s, 2)
                for h in range(H):
                    for t in range(T):
                        pe.matmul(acc[:, h, t * P:(t + 1) * P], b_v[:, t, h * P:(h + 1) * P], b_at[:, h, t, :], start=True, stop=False, skip_group_check=True)
                        for c in range(max(4 * t, 1), 4 * t + 4):
                            s = slice(c * HGC, (c + 1) * HGC)
                            ins = pe.matmul(acc[:, h, s], b_s[:, c - 1, h, :], b_q[:, h, s], start=False, stop=(c == 4 * t + 3), skip_group_check=True)
                    ins.then_inc(hg_o, 1)
                slot(0, 9)
                for h in range(H):
                    pe.wait_ge(hg_oc, h + 1)
                    pe.matmul(acc[:, h, 0:S], ones, b_sq[:, h, :], start=True, stop=True).then_inc(hg_ss, 1)
                for s in range(10, 14):
                    slot(0, s)
                pe.wait_ge(hg_rs, H)
                for s in range(3):
                    out_slot(0, s, (1, 1, 2)[s])
                out_slot(0, 3, 3)
                close()

            def close():
                for b in range(4):
                    ins = pe.matmul(acc[:, b, :], zb[:, 0:P], zb[:, :], start=False, stop=True, skip_group_check=True)
                ins.then_inc(acc_done, 1)

            def mixer_cd():
                slot(1, 0)
                pe.wait_ge(fg_in, 64)
                for k in range(KD):
                    ins = pe.matmul(acc[0:36, 0, 0:S], wgate[:, k, :], act[:, k, :], start=(k == 0), stop=(k == KD - 1))
                ins.then_inc(gt_mm, 1)
                slot(1, 1)
                slot(1, 2)
                pe.wait_ge(gt_rows, 1)
                for t in range(T):
                    ins = pe.transpose(acc[:, 0, t * H:(t + 1) * H], row[:, 5, t * P:(t + 1) * P], ident[0:H, 0:H])
                ins.then_inc(gt_tp, 1)
                slot(1, 3)
                pe.wait_ge(gt_col, 1)
                sel = const("sel").rearrange("p (h m) -> p h m", h=H)
                for h in range(H):
                    pe.matmul(acc[:, h, :], sel[0:H, h, :], row[:, 6:8, :].rearrange("p n s -> p (n s)"), start=True, stop=True).then_inc(gt_bc, 1)
                slot(1, 4)
                pe.wait_ge(gt_dt, H)
                pe.wait_ge(chunk_out, CHUNKS + 8)
                for n, buf in enumerate((c_q, c_k)):
                    for half in range(2):
                        pe.matmul(acc[:, 2 * n + half, :], const("rot"), buf[:, 2 * half:2 * half + 2, :].rearrange("p h s -> p (h s)"),
                                  start=True, stop=True).then_inc(mb_rot, 1)
                slot(1, 5)
                slot(1, 6)
                pe.wait_ge(mb_qk, 2)
                for h in range(H):
                    pe.matmul(acc[:, h, 0:P], c_q[:, h, 0:P], c_k[:, h, 0:P], start=True, stop=True)
                    pe.matmul(acc[:, h, P:384], c_q[:, h, P:S], c_k[:, h, :], start=True, stop=True).then_inc(mb_s, 1)
                slot(1, 7)
                for h in range(H):
                    pe.wait_ge(mb_pn, h + 1)
                    for b in range(3):
                        ins = pe.transpose(acc[:, h, b * P:(b + 1) * P], c_p[:, h, b * P:(b + 1) * P], ident)
                    ins.then_inc(mb_pt, 1)
                slot(1, 8)
                for h in range(H):
                    pe.wait_ge(mb_ptc, h + 1)
                    g = slice(h * P, (h + 1) * P)
                    pe.matmul(acc[:, h, 0:S], c_v[:, 0, g], c_pt[:, h, 0:S], start=True, stop=False, skip_group_check=True)
                    pe.matmul(acc[:, h, P:S], c_v[:, 1, g], c_pt[:, h, S:384], start=False, stop=True, skip_group_check=True).then_inc(mb_o, 1)
                slot(1, 9)
                slot(1, 10)
                pe.wait_ge(y_f, 3 + H)
                pe.wait_ge(chunk_out, CHUNKS + 20)
                for h in range(H):
                    pe.matmul(acc[:, h, 0:S], c_lk[:, h, 0:P], c_lq[:, h, :], start=True, stop=True)
                    pe.matmul(acc[:, h, S:384], c_lk[:, h, P:S], c_lq[:, h, P:S], start=True, stop=True).then_inc(ml_s, 1)
                slot(1, 11)
                slot(1, 12)
                pe.wait_ge(chunk_out, CHUNKS + 24)
                for h in range(H):
                    pe.wait_ge(ml_w, h + 1)
                    g = slice(h * P, (h + 1) * P)
                    for lhs, at in (((c_lv[:, 0, g], c_lv[:, 1, g]), 0), ((ones, ones), S)):
                        pe.matmul(acc[:, h, at:at + S], lhs[0], c_dt[:, h, 0:S], start=True, stop=False, skip_group_check=True)
                        ins = pe.matmul(acc[:, h, at + P:at + S], lhs[1], c_dt[:, h, S:384], start=False, stop=True, skip_group_check=True)
                    ins.then_inc(ml_n, 1)
                slot(1, 13)
                pe.wait_ge(ml_h, H)
                out_slot(1, 0, 4)
                pe.wait_ge(chunk_out, 2 * CHUNKS)
                for h in range(H):
                    pe.wait_ge(ml_sq, h + 1)
                    pe.matmul(ch[:, h, 0:S], ones, c_sq[:, h, :], start=True, stop=True).then_inc(ml_ss, 1)
                out_slot(1, 1, 4)
                out_slot(1, 2, 5)
                out_slot(1, 3, 6)
                close()

            pe.wait_ge(const_in, 16)
            pe.wait_ge(small_in, 7 * 16)
            pe.wait_ge(setup, 4)
            pe.transpose(ch[:, 0, 0:N_ROWS], prow[0:N_ROWS, :], ident[0:N_ROWS, 0:N_ROWS]).then_inc(prow_t, 1)
            pe.wait_ge(pcol_done, 1)
            m = 0
            for kind, f in PHASES:
                norm(m)
                if kind == "ffn":
                    if m:
                        pe.wait_ge(x_ready, 2 * m + 2)
                m += 1
                pe.wait_ge(xl_ready, 4 * m)
                if kind == "ffn":
                    ffn(f, m)
                elif kind == "ab":
                    mixer_ab()
                else:
                    mixer_cd()


_INS = ["x", "ffn_norm", "ffn_w_in", "ffn_w_out", "mix_norm", "ab_w_in", "ab_w_out", "hgrn_lb_logits", "hgrn_out_norm",
        "conv_w", "conv_b", "cd_w_in", "cd_w_out", "mlstm_gate_bias", "mlstm_out_norm", "final_norm"]


def kernel(**inputs):
    import concourse.bacc as bacc
    from concourse.bass_utils import run_bass_kernel_spmd

    nc = bacc.Bacc("TRN2", target_bir_lowering=False, num_devices=1)
    arrays = {f"in_{n}": np.ascontiguousarray(inputs[n]) for n in _INS}
    arrays["in_consts"] = shape_constants()
    args = [nc.dram_tensor(n, a.shape, mybir.dt.from_np(a.dtype), kind="ExternalInput").ap() for n, a in arrays.items()]
    args.append(nc.dram_tensor("out_0", (1, S, D), F32, kind="ExternalOutput").ap())
    build(nc, *args)
    r = run_bass_kernel_spmd(nc, [arrays], core_ids=[0])
    return r.results[0]["out_0"]
```

```python
from contextlib import ExitStack

import numpy as np

import concourse.bass as bass
from concourse import mybir

F32 = mybir.dt.float32
F32R = mybir.dt.float32r
BF16 = mybir.dt.bfloat16
ALU = mybir.AluOpType
ACT = mybir.ActivationFunctionType
AX = mybir.AxisListType

P = 128
D = 1024
S = 256
T = S // P
KD = D // P
F = 2816
G = 512
H = G // P
PAIR = 2 * P
SLOT = KD * PAIR
ITER = F // PAIR
RING = 3
NMIX = 18
HGC = 32
EPS = 1e-6
ROOT_D = 32.0
MASKED = -1e30

FFN_BASE = [0, 3 * ITER + NMIX, 6 * ITER + NMIX, 9 * ITER + 2 * NMIX]
MIX_BASE = [3 * ITER, 9 * ITER + NMIX]
SLOTS = 12 * ITER + 2 * NMIX
OUT_FFN = [0, ITER + 2, 2 * ITER + 1, 3 * ITER + 3]
OUT_MIX = [ITER - 1, 3 * ITER]
PHASES = [("ffn", 0), ("ab", 0), ("ffn", 1), ("ffn", 2), ("cd", 1), ("ffn", 3)]
FIRST_SLOT = [(FFN_BASE if kind == "ffn" else MIX_BASE)[f] for kind, f in PHASES]
CHUNKS = 28

C_FFN, C_MIX, C_HGN, C_CW, C_CB, C_MLN, C_LB, N_ROWS = 0, 32, 48, 52, 64, 68, 72, 84

CONST = dict(ident=128, ones=128, m_ij=384, m_ji=384, bd=128, reset=256, cos=256, sin=256, rot=128, sel=512)
C_AT = {}
for _n, _w in CONST.items():
    C_AT[_n] = sum(CONST[m] for m in list(CONST)[:list(CONST).index(_n)])
N_CONST = sum(CONST.values())


def shape_constants():
    a = np.arange(P)
    c = {}
    c["ident"] = np.eye(P)
    c["ones"] = np.ones((P, P))
    low = np.where(a[None, :] <= a[:, None], 0.0, MASKED)
    zero = np.zeros((P, P))
    c["m_ij"] = np.concatenate([low, zero, low], 1)
    c["m_ji"] = np.concatenate([low.T, zero, low.T], 1)
    c["bd"] = ((a[:, None] // HGC == a[None, :] // HGC) & (a[:, None] <= a[None, :])).astype(float)
    c["reset"] = np.tile((np.arange(S) % HGC != 0).astype(float), (P, 1))
    half = P // 4 // 2
    inv = np.float32(500000.0) ** (-np.arange(half, dtype=np.float32) * np.float32(2.0) / np.float32(2 * half))
    ang = np.arange(S, dtype=np.float32)[None, :] * inv[:, None].astype(np.float32)
    c["cos"] = np.concatenate([np.cos(ang), np.cos(ang), np.ones((P - 2 * half, S))], 0)
    c["sin"] = np.concatenate([np.sin(ang), np.sin(ang), np.zeros((P - 2 * half, S))], 0)
    rot = np.zeros((P, P))
    for d in range(half):
        rot[d + half, d] = -1.0
        rot[d, d + half] = 1.0
    c["rot"] = rot
    sel = np.zeros((P, H, P))
    for h in range(H):
        sel[h, h, :] = 1.0
    c["sel"] = sel.reshape(P, H * P)
    return np.ascontiguousarray(np.concatenate([c[n] for n in CONST], 1).astype(np.float32))


def build(nc, x, ffn_norm, ffn_w_in, ffn_w_out, mix_norm, ab_w_in, ab_w_out, hgrn_lb_logits, hgrn_out_norm,
          conv_w, conv_b, cd_w_in, cd_w_out, mlstm_gate_bias, mlstm_out_norm, final_norm, consts, out):
    ctx = ExitStack()
    with ctx:
        def sb(name, shape, dt=F32):
            return ctx.enter_context(nc.sbuf_tensor(name, shape, dt))

        def sem(name):
            return ctx.enter_context(nc.semaphore(name))

        raw = sb("raw", [P, RING, SLOT])
        w_hi = sb("w_hi", [P, RING, SLOT], F32R)
        w_lo = sb("w_lo", [P, RING, SLOT], F32R)
        xs = sb("xs", [P, T, D])
        xn = sb("xn", [P, T, D])
        act = sb("act", [P, KD, S])
        x_hi = sb("x_hi", [P, KD, S], F32R)
        x_lo = sb("x_lo", [P, KD, S], F32R)
        y_hi = sb("y_hi", [P, KD, S], F32R)
        y_lo = sb("y_lo", [P, KD, S], F32R)
        mix = sb("mix", [P, 15, H * S])
        cst = sb("cst", [P, N_CONST])
        prow = sb("prow", [P, P])
        pcol = sb("pcol", [P, N_ROWS])
        fgain = sb("fgain", [P, D])
        gbias = sb("gbias", [H, 2])
        wgate = sb("wgate", [P, KD, 36])
        zb = sb("zb", [P, 512], BF16)
        col = sb("col", [P, 64])

        ch = ctx.enter_context(nc.psum_tensor("ch", [P, 4, 512], F32))
        acc = ctx.enter_context(nc.psum_tensor("acc", [P, 4, 512], F32))

        def const(name):
            return cst[:, C_AT[name]:C_AT[name] + CONST[name]]

        ident, ones = const("ident"), const("ones")
        eps_c, one_c = col[:, 0:1], col[:, 1:2]
        half_c, ssq, lnv, rstd = col[:, 63:64], col[:, 2:6], col[:, 6:8], col[:, 56:58]
        lb, oml = col[:, 8:12], col[:, 12:16]
        lbt, lbe = col[:, 16:20], col[:, 20:32]
        gcol = col[:, 32:40]
        nmax, rsum = col[:, 40:48], col[:, 48:56]

        def gain(at):
            return pcol[:, at:at + 1]

        def m4(n):
            return mix[:, n, :].rearrange("p (h s) -> p h s", h=H)

        f_sig = mix[:, 1, 0:2 * S].rearrange("p (j s) -> p j s", j=2)
        b_f, b_lf, b_b, b_eb, b_kc, b_kd = (m4(n) for n in range(6))
        b_q = m4(7)
        b_kt = mix[:, 0, :].rearrange("p (h t d) -> p h t d", h=H, t=T)
        b_at = mix[:, 1, :].rearrange("p (h t d) -> p h t d", h=H, t=T)
        b_v = mix[:, 8, :].rearrange("p (t c) -> p t c", t=T)
        b_s = mix[:, 9:13, :].rearrange("p n c -> p (n c)")[:, 0:7 * G].rearrange("p (c h v) -> p c h v", c=7, h=H)
        b_g = m4(13)
        b_c, b_z = m4(14), mix[:, 2:4, :].rearrange("p n c -> p (n c)")[:, 0:H * (S + 2)].rearrange("p (h s) -> p h s", h=H)
        b_o, b_sq = xn[:, 0, :].rearrange("p (h s) -> p h s", h=H), xn[:, 1, :].rearrange("p (h s) -> p h s", h=H)
        b_u, b_bg, b_rs = m4(5), m4(4), m4(7)
        c_q, c_k, c_lk, c_lq = m4(0), m4(1), m4(3), m4(4)
        c_v = mix[:, 2, :].rearrange("p (t c) -> p t c", t=T)
        c_lv = mix[:, 5, :].rearrange("p (t c) -> p t c", t=T)
        c_dt = mix[:, 6:8, :].rearrange("p n c -> p (n c)")[:, 0:H * 384].rearrange("p (h c) -> p h c", h=H)
        c_em = m4(8)
        c_p = mix[:, 9:11, :].rearrange("p n c -> p (n c)")[:, 0:H * 384].rearrange("p (h c) -> p h c", h=H)
        c_rs = mix[:, 9:11, :]
        c_pt = mix[:, 11:13, :].rearrange("p n c -> p (n c)")[:, 0:H * 384].rearrange("p (h c) -> p h c", h=H)
        c_oe, c_h, c_sq = m4(13), m4(14), m4(9)
        c_rn = m4(11)
        row = mix[0:H, 11:13, :].rearrange("p n c -> p (n c)").rearrange("p (n s) -> p n s", s=S)

        slot_in = [sem(f"slot_in{r}") for r in range(RING)]
        hi_done = sem("hi_done")
        lo_done = sem("lo_done")
        out_used = sem("out_used")
        ident_in = sem("ident_in")
        small_in, x_in, const_in, fg_in = sem("small_in"), sem("x_in"), sem("const_in"), sem("fg_in")
        setup = sem("setup")
        prow_t, pcol_done = sem("prow_t"), sem("pcol_done")
        lb_sub, lb_exp = sem("lb_sub"), sem("lb_exp")
        dve, actq = sem("dve_order"), sem("act_order")
        x_ready = sem("x_ready")
        ssq_ready = sem("ssq_ready")
        rstd_ready = sem("rstd_ready")
        pool_order = sem("pool_order")
        xn_ready = sem("xn_ready")
        tp_ready = sem("tp_ready")
        xt_ready, xh_ready, xl_ready = sem("xt_ready"), sem("xh_ready"), sem("xl_ready")
        gate_ready, up_ready, gate_silu = sem("gate_ready"), sem("up_ready"), sem("gate_silu")
        hid, hid_hi, hid_lo = sem("hid"), sem("hid_hi"), sem("hid_lo")
        acc_done = sem("acc_done")
        chunk, chunk_out = sem("chunk"), sem("chunk_out")
        y_f, y_h, y_l = sem("y_f"), sem("y_h"), sem("y_l")
        f_ready, lf_ready, b_ready, e_ready, kd_ready, q_ready = (sem(n) for n in ("f_ready", "lf_ready", "b_ready", "e_ready", "kd_ready", "q_ready"))
        hg_at, hg_ev, hg_ds, hg_s, hg_o, hg_oc, hg_ss, hg_rs = (sem(n) for n in ("hg_at", "hg_ev", "hg_ds", "hg_s", "hg_o", "hg_oc", "hg_ss", "hg_rs"))
        gt_mm, gt_na, gt_ln, gt_rows, gt_tp, gt_col, gt_bc, gt_pre, gt_dt = (sem(n) for n in ("gt_mm", "gt_na", "gt_ln", "gt_rows", "gt_tp", "gt_col", "gt_bc", "gt_pre", "gt_dt"))
        mb_rot, mb_cos, mb_qk, mb_s, mb_sm, mb_p, mb_pn, mb_pt, mb_ptc, mb_o = (sem(n) for n in ("mb_rot", "mb_cos", "mb_qk", "mb_s", "mb_sm", "mb_p", "mb_pn", "mb_pt", "mb_ptc", "mb_o"))
        ml_s, ml_w, ml_n, ml_h, ml_sq, ml_ss, ml_ar, ml_rs = (sem(n) for n in ("ml_s", "ml_w", "ml_n", "ml_h", "ml_sq", "ml_ss", "ml_ar", "ml_rs"))
        y_out, out_done = sem("y_out"), sem("out_done")

        def slot3(t, r):
            return t[:, r, :].rearrange("p (k n) -> p k n", k=KD)

        def slot2(t, r):
            return t[:, r, :].rearrange("p (r n) -> p r n", r=2)

        AB_COLS = [(1, 0), (1, 1), (2, 0), (2, 1), (0, 0), (0, 1), (3, 0), (3, 1), (5, 0), (5, 1), (6, 0), (6, 1), (4, 0), (4, 1)]
        CD_COLS = [(3, 0), (3, 1), (0, 0), (0, 1), (1, 0), (1, 1), (2, 0), (2, 1), (4, 0), (4, 1), (5, 0), (5, 1), (6, 0), (6, 1)]
        AB_ROWS, CD_ROWS = [0, 2, 4, 6], [0, 2, 4, 6]
        TOK = (2, 3), (6, 7, 12, 13)

        block = ctx.enter_context(nc.Block())

        @block.sync
        def _(sp):
            for t in range(T):
                sp.dma_start(xs[:, t, :], x[0, t * P:(t + 1) * P, :]).then_inc(x_in, 16)

            def load(pos, n, dst, src, first=False):
                if not first:
                    sp.wait_ge(lo_done, n - (RING - 1))
                sp.dma_start(dst, src).then_inc(slot_in[pos], 16)

            def ffn(f, at):
                win, wout = ffn_w_in[f // 2, f % 2], ffn_w_out[f // 2, f % 2]

                def step(i, first=False):
                    n = FFN_BASE[f] + 3 * i
                    for kind in range(2):
                        load(kind, n + kind, slot3(raw, kind),
                             win[:, bass.ds(kind * F + i * PAIR, PAIR)].rearrange("(k p) n -> p k n", p=P), first)
                    load(2, n + 2, slot2(raw, 2),
                         wout[bass.ds(i * PAIR, PAIR), :].rearrange("(r p) n -> p r n", p=P), first)

                if f == 0:
                    step(0, True)
                    sp.dma_start(cst[:, P:N_CONST], consts[:, P:N_CONST]).then_inc(const_in, 16)
                with sp.Fori(1 if f == 0 else 0, ITER) as i:
                    step(i)

            def mixer(m):
                win, wout = (ab_w_in, cd_w_in)[m][0], (ab_w_out, cd_w_out)[m][0]
                for s in range(14):
                    g, half = (AB_COLS, CD_COLS)[m][s]
                    c0 = g * G + half * PAIR + (2 * H if m == 1 and g >= 4 else 0)
                    n = MIX_BASE[m] + s
                    load(n % RING, n, slot3(raw, n % RING), win[:, c0:c0 + PAIR].rearrange("(k p) n -> p k n", p=P))
                for s in range(4):
                    r0 = (AB_ROWS, CD_ROWS)[m][s] * P
                    n = MIX_BASE[m] + 14 + s
                    load(n % RING, n, slot2(raw, n % RING), wout[r0:r0 + PAIR, :].rearrange("(r p) n -> p r n", p=P))

            for kind, f in PHASES:
                if kind == "ffn":
                    ffn(f, f)
                else:
                    mixer(f)
            for t in range(T):
                sp.wait_ge(y_out, t + 1)
                sp.dma_start(out[0, t * P:(t + 1) * P, :], xn[:, t, :]).then_inc(out_done, 16)
            sp.wait_ge(out_done, 16 * T)

        @block.gpsimd
        def _(pool):
            pool.memset(zb[:, :], 0.0).then_inc(setup, 1)
            pool.memset(eps_c, EPS).then_inc(setup, 1)
            pool.memset(one_c, 1.0).then_inc(setup, 1)
            pool.memset(half_c, -0.5).then_inc(setup, 1)
            pool.memset(wgate[:, :, :], 0.0).then_inc(setup, 1)
            pool.dma_start(fgain[:, :], final_norm.rearrange("(a n) -> a n", a=1).broadcast_to([P, D])).then_inc(fg_in, 16)
            pool.wait_ge(setup, 5)
            with nc.allow_non_contiguous_dma(reason="eight columns of gate weights, eight biases"):
                for j in range(2):
                    pool.dma_start(wgate[:, :, 32 * j:32 * j + H],
                                   cd_w_in[0][:, 4 * G + H * j:4 * G + H * j + H].rearrange("(k p) n -> p k n", p=P)).then_inc(fg_in, 16)
                pool.dma_start(gbias[:, :], mlstm_gate_bias[0].rearrange("j h -> h j")).then_inc(fg_in, 16)
            for m in range(7):
                for t in range(T):
                    n = 2 * m + t
                    pool.wait_ge(ssq_ready, n + 1)
                    pool.tensor_scalar(lnv[:, t:t + 1], ssq[:, 2 * t:2 * t + 1], ssq[:, 2 * t + 1:2 * t + 2], EPS * D, ALU.add, ALU.add).then_inc(pool_order, 1)
                    pool.wait_ge(pool_order, n + 1)
                    pool.tensor_tensor(rstd[:, t:t + 1], lnv[:, t:t + 1], half_c, ALU.pow).then_inc(rstd_ready, 1)
                if m == 4:
                    pool.wait_ge(const_in, 16)
                    cos = const("cos").unsqueeze(1).broadcast_to([P, H, S])
                    for n, buf in enumerate((c_q, c_k)):
                        pool.wait_ge(mb_rot, 2 * n + 2)
                        pool.tensor_tensor(buf[:, :, :], buf[:, :, :], cos, ALU.mult).then_inc(mb_cos, 1)

        @block.scalar
        def _(ae):
            def loads():
                ae.dma_start(cst[:, 0:P], consts[:, 0:P]).then_inc(ident_in, 16)
                for at, src in ((C_FFN, ffn_norm.rearrange("l j (k p) -> (l j k) p", p=P)),
                                (C_MIX, mix_norm.rearrange("l (k p) -> (l k) p", p=P)),
                                (C_HGN, hgrn_out_norm[0]),
                                (C_CW, conv_w[0].rearrange("w (h p) -> (w h) p", p=P)),
                                (C_CB, conv_b[0].rearrange("(h p) -> h p", p=P)),
                                (C_MLN, mlstm_out_norm[0]),
                                (C_LB, hgrn_lb_logits.rearrange("r (h p) -> (r h) p", p=P))):
                    ae.dma_start(prow[at:at + src.shape[0], :], src).then_inc(small_in, 16)

            order = [0]

            def own(ins):
                order[0] += 1
                ins.then_inc(actq, 1)
                ae.wait_ge(actq, order[0])

            def round_slot(pos, landed):
                ae.wait_ge(slot_in[pos], landed)
                ae.activation(w_hi[:, pos, :], raw[:, pos, :], ACT.Copy).then_inc(hi_done, 1)

            def split_out(f, i):
                n = FFN_BASE[f] + 2
                ae.wait_ge(out_used, OUT_FFN[f] + i)
                round_slot(n % RING, 16 * (n // RING + 1) + 16 * i)

            def split_in(f, i, kind):
                n = FFN_BASE[f] + RING + kind
                ae.wait_ge((gate_ready, up_ready)[kind], 2 * ITER * f + 2 * i + 2)
                round_slot(n % RING, 16 * (n // RING + 1) + 16 * i)

            def norm(m):
                for t in range(T):
                    for half in range(2):
                        ae.wait_ge(x_ready, 4 * m + 2 * t + half + 1)
                        c = slice(512 * half, 512 * half + 512)
                        ins = ae.activation(xn[:, t, c], xs[:, t, c], ACT.Square, accum_out=ssq[:, 2 * t + half:2 * t + half + 1])
                    ins.then_inc(ssq_ready, 1)
                if m == 6:
                    return
                if m == 0:
                    round_slot(0, 16)
                for b in range(4):
                    t, half = b // 2, b % 2
                    sl = (slice(None), slice(4 * half, 4 * half + 4), slice(t * P, (t + 1) * P))
                    ae.wait_ge(xt_ready, 4 * m + b + 1)
                    ae.activation(x_hi[sl], act[sl], ACT.Copy).then_inc(xh_ready, 1)

            def ffn(f):
                def step(i, last=False, f_first=False):
                    q0 = 2 * ITER * f + 2 * i

                    def hidden(j):
                        ae.wait_ge(hid, q0 + j + 1)
                        ae.activation(y_hi[:, j, :], act[:, j, :], ACT.Copy).then_inc(hid_hi, 1)

                    if not f_first:
                        split_out(f, i)
                    for j in range(2):
                        ae.wait_ge(gate_ready, q0 + j + 1)
                        ae.activation(f_sig[:, j, :], ch[:, 2 * j, 0:S], ACT.Silu).then_inc(gate_silu, 1)
                        if j == 0:
                            hidden(0)
                    if not last:
                        split_in(f, i, 0)
                    hidden(1)
                    if not last:
                        split_in(f, i, 1)

                if f == 0:
                    step(0, f_first=True)
                with ae.Fori(1 if f == 0 else 0, ITER - 1 if f == 3 else ITER) as i:
                    step(i)
                if f == 3:
                    step(ITER - 1, last=True)

            def after(m, s):
                if s < 0:
                    ae.wait_ge(out_used, OUT_MIX[m])
                elif s < 14:
                    ae.wait_ge(chunk, CHUNKS * m + 2 * s + 2)
                else:
                    ae.wait_ge(out_used, OUT_MIX[m] + s - 13)
                n = MIX_BASE[m] + s + RING
                round_slot(n % RING, 16 * (n // RING + 1))

            def chunks(m, s, *moves):
                for j in range(2):
                    c = 2 * s + j
                    ae.wait_ge(chunk, CHUNKS * m + c + 1)
                    src = ch[:, c % 4, 0:S]
                    for k, (dst, func, scale) in enumerate(moves):
                        ins = ae.activation(dst(j), src, func, scale=scale)
                    ins.then_inc(chunk_out, 1)
                after(m, s)

            def y_split(parts):
                for k0, k1, count in parts:
                    ae.wait_ge(y_f, count)
                    ae.activation(y_hi[:, k0:k1, :], act[:, k0:k1, :], ACT.Copy).then_inc(y_h, 1)

            def mixer_ab():
                after(0, -1)
                for s in (0, 1):
                    chunks(0, s, (lambda j: b_f[:, 2 * s + j, :], ACT.Tanh, 0.5))
                ae.preload_act_table_set("natural_log_exp_and_others")
                ae.wait_ge(lb_sub, 1)
                ae.activation(lbe, lbe, ACT.Exp).then_inc(lb_exp, 1)
                for p in range(2):
                    ae.wait_ge(f_ready, p + 1)
                    ae.activation(b_lf[:, 2 * p:2 * p + 2, :], b_f[:, 2 * p:2 * p + 2, :], ACT.Ln).then_inc(lf_ready, 1)
                chunks(0, 2, (lambda j: b_v[:, j, 0:PAIR], ACT.Copy, 1.0))
                for p in range(2):
                    h = slice(2 * p, 2 * p + 2)
                    ae.wait_ge(b_ready, p + 1)
                    ae.activation(b_lf[:, h, :], b_lf[:, h, :], ACT.Exp)
                    own(ae.activation(b_eb[:, h, :], b_b[:, h, :], ACT.Exp))
                    ae.activation(b_b[:, h, :], b_b[:, h, :], ACT.Exp, scale=-1.0).then_inc(e_ready, 1)
                chunks(0, 3, (lambda j: b_v[:, j, PAIR:2 * PAIR], ACT.Copy, 1.0))
                ae.preload_act_table_set("silu_and_others")
                for s in (4, 5):
                    chunks(0, s, (lambda j: b_q[:, 2 * s - 8 + j, :], ACT.Silu, 1.0))
                for s in (6, 7):
                    chunks(0, s, (lambda j: b_g[:, 2 * s - 12 + j, :], ACT.Silu, 1.0))
                ae.preload_act_table_set("natural_log_exp_and_others")
                for s in (8, 9):
                    chunks(0, s, (lambda j: b_c[:, 2 * s - 16 + j, :], ACT.Copy, 1.0))
                for h in range(H):
                    ae.wait_ge(hg_o, h + 1)
                    ae.activation(b_o[:, h, :], acc[:, h, 0:S], ACT.Copy)
                    ae.activation(b_sq[:, h, :], acc[:, h, 0:S], ACT.Square).then_inc(hg_oc, 1)
                chunks(0, 10, (lambda j: b_u[:, j, :], ACT.Copy, 1.0))
                for h in range(H):
                    ae.wait_ge(hg_ss, h + 1)
                    own(ae.activation(b_rs[:, h, :], acc[:, h, 0:S], ACT.Ln, bias=eps_c, scale=1.0 / P))
                    ae.activation(b_rs[:, h, :], b_rs[:, h, :], ACT.Exp, scale=-0.5).then_inc(hg_rs, 1)
                ae.preload_act_table_set("silu_and_others")
                chunks(0, 11, (lambda j: b_u[:, 2 + j, :], ACT.Copy, 1.0))
                for s in (12, 13):
                    chunks(0, s, (lambda j: b_bg[:, 2 * s - 24 + j, :], ACT.Copy, 1.0))
                    y_split(([(0, 4, 1), (4, 6, 2)], [(6, 8, 3)])[s - 12])
                for s in (14, 15, 16):
                    after(0, s)

            def mixer_cd():
                after(1, -1)
                for s in (0, 1):
                    chunks(1, s, (lambda j: c_oe[:, 2 * s + j, :], ACT.Tanh, 0.5))
                ae.preload_act_table_set("natural_log_exp_and_others")
                ae.wait_ge(gt_na, 1)
                own(ae.activation(row[:, 2, :], row[:, 2, :], ACT.Exp))
                ae.activation(row[:, 3, :], row[:, 2, :], ACT.Ln, bias=one_c[0:H, :]).then_inc(gt_ln, 1)
                for s in (2, 3):
                    chunks(1, s, (lambda j: c_lq[:, 2 * s - 4 + j, :], ACT.Copy, P ** -0.5))
                for h in range(H):
                    ae.wait_ge(gt_pre, h + 1)
                    ae.activation(c_em[:, h, :], acc[:, h, S:2 * S], ACT.Exp)
                    ae.activation(c_dt[:, h, 0:S], c_dt[:, h, 0:S], ACT.Exp, bias=gcol[:, h:h + 1])
                    ae.activation(c_dt[:, h, S:384], c_dt[:, h, S:384], ACT.Exp, bias=gcol[:, H + h:H + h + 1]).then_inc(gt_dt, 1)
                for s in (4, 5):
                    chunks(1, s, (lambda j: c_lk[:, 2 * s - 8 + j, :], ACT.Copy, 1.0))
                for s in (6, 7):
                    chunks(1, s, (lambda j: c_lv[:, j, (s - 6) * PAIR:(s - 5) * PAIR], ACT.Copy, 1.0))
                chunks(1, 8, (lambda j: c_q[:, j, :], ACT.Copy, 1.0))
                for h in range(H):
                    ae.wait_ge(ml_h, h + 1)
                    ae.activation(c_h[:, h, :], acc[:, h, 0:S], ACT.Copy)
                    ae.activation(c_sq[:, h, :], acc[:, h, 0:S], ACT.Square).then_inc(ml_sq, 1)
                chunks(1, 9, (lambda j: c_q[:, 2 + j, :], ACT.Copy, 1.0))
                for h in range(H):
                    ae.wait_ge(ml_ar, h + 1)
                    own(ae.activation(c_rn[:, h, :], c_rn[:, h, :], ACT.Ln))
                    ae.activation(c_rn[:, h, :], c_rn[:, h, :], ACT.Exp, scale=-0.5).then_inc(ml_rs, 1)
                for s in (10, 11):
                    chunks(1, s, (lambda j: c_k[:, 2 * s - 20 + j, :], ACT.Copy, 1.0))
                    y_split([(2 * s - 20, 2 * s - 18, s - 6)])
                chunks(1, 12, (lambda j: c_v[:, j, 0:PAIR], ACT.Copy, 1.0))
                for h in range(H):
                    ae.wait_ge(mb_sm, h + 1)
                    ae.activation(c_p[:, h, 0:P], c_p[:, h, 0:P], ACT.Exp, bias=nmax[:, 2 * h:2 * h + 1],
                                  scale=P ** -0.5, accum_out=rsum[:, 2 * h:2 * h + 1])
                    ae.activation(c_p[:, h, P:384], c_p[:, h, P:384], ACT.Exp, bias=nmax[:, 2 * h + 1:2 * h + 2],
                                  scale=P ** -0.5, accum_out=rsum[:, 2 * h + 1:2 * h + 2]).then_inc(mb_p, 1)
                chunks(1, 13, (lambda j: c_v[:, j, PAIR:2 * PAIR], ACT.Copy, 1.0))
                ae.preload_act_table_set("silu_and_others")
                for h in range(H):
                    ae.wait_ge(mb_pt, h + 1)
                    ae.activation(c_pt[:, h, :], ch[:, h, 0:384], ACT.Copy).then_inc(mb_ptc, 1)
                after(1, 14)
                for p in range(2):
                    for h in (2 * p, 2 * p + 1):
                        ae.wait_ge(mb_o, h + 1)
                        ae.activation(act[:, 4 + h, :], ch[:, h, 0:S], ACT.Copy).then_inc(y_f, 1)
                    y_split([(4 + 2 * p, 6 + 2 * p, 7 + 2 * p)])
                for s in (15, 16):
                    after(1, s)

            loads()
            ae.preload_act_table_set("silu_and_others")
            ae.wait_ge(setup, 4)
            m = 0
            for kind, f in PHASES:
                norm(m)
                if m == 0:
                    for n in range(1, RING):
                        round_slot(n, 16)
                m += 1
                if kind == "ffn":
                    ffn(f)
                elif kind == "ab":
                    mixer_ab()
                else:
                    mixer_cd()
            norm(6)

        @block.vector
        def _(v):
            order = [0]

            def own(ins):
                order[0] += 1
                ins.then_inc(dve, 1)
                v.wait_ge(dve, order[0])

            def rest(n, pos, wait_used=True):
                v.wait_ge(hi_done, n + 1)
                v.tensor_tensor(w_lo[:, pos, :], raw[:, pos, :], w_hi[:, pos, :].bitcast(F32), ALU.subtract).then_inc(lo_done, 1)

            def residual(m, scale, t):
                if m:
                    v.wait_ge(acc_done, 2 * (m - 1) + t + 1)
                    for half in range(2):
                        dst = xs[:, t, 512 * half:512 * half + 512]
                        v.scalar_tensor_tensor(out=dst, in0=acc[:, 2 * t + half, :], scalar=scale, in1=dst, op0=ALU.mult, op1=ALU.add).then_inc(x_ready, 1)

            def norm(m, gains, scale):
                def scaled(t):
                    v.wait_ge(rstd_ready, 2 * m + t + 1)
                    v.wait_ge(x_ready, 4 * m + 2 * t + 2)
                    v.tensor_scalar(xn[:, t, :], xs[:, t, :], rstd[:, t:t + 1], ROOT_D, ALU.mult, ALU.mult).then_inc(xn_ready, 1)

                def gained(b):
                    t, half = b // 2, b % 2
                    v.wait_ge(tp_ready, 4 * m + b + 1)
                    g = pcol[:, gains + 4 * half:gains + 4 * half + 4].unsqueeze(2).broadcast_to([P, 4, P])
                    v.tensor_tensor(act[:, 4 * half:4 * half + 4, t * P:(t + 1) * P],
                                    ch[:, b, :].rearrange("p (k s) -> p k s", k=4), g, ALU.mult).then_inc(xt_ready, 1)

                def low(b):
                    t, half = b // 2, b % 2
                    sl = (slice(None), slice(4 * half, 4 * half + 4), slice(t * P, (t + 1) * P))
                    v.wait_ge(xh_ready, 4 * m + b + 1)
                    v.tensor_tensor(x_lo[sl], act[sl], x_hi[sl].bitcast(F32), ALU.subtract).then_inc(xl_ready, 1)

                residual(m, scale, 0)
                residual(m, scale, 1)
                scaled(0)
                scaled(1)
                if m == 0:
                    rest(0, 0)
                gained(0)
                gained(1)
                low(0)
                low(1)
                gained(2)
                gained(3)
                low(2)
                low(3)
                n = FIRST_SLOT[m] + 1
                rest(n, n % RING)
                if m == 0:
                    rest(2, 2)

            def ffn(f):
                def step(i, last=False, late=False, f_first=False):
                    q0 = 2 * ITER * f + 2 * i
                    n0 = FFN_BASE[f] + 3 * i

                    def hidden(j):
                        v.wait_ge(gate_silu, q0 + j + 1)
                        v.wait_ge(up_ready, q0 + j + 1)
                        v.tensor_tensor(act[:, j, :], ch[:, 2 * j + 1, 0:S], f_sig[:, j, :], ALU.mult).then_inc(hid, 1)
                        v.wait_ge(hid_hi, q0 + j + 1)
                        v.tensor_tensor(y_lo[:, j, :], act[:, j, :], y_hi[:, j, :].bitcast(F32), ALU.subtract).then_inc(hid_lo, 1)

                    if not f_first:
                        rest(n0 + 2, 2)
                    hidden(0)
                    hidden(1)
                    if not last:
                        rest(n0 + 3, 0)
                        if not late:
                            rest(n0 + 4, 1)

                if f == 0:
                    step(0, f_first=True)
                with v.Fori(1 if f == 0 else 0, ITER - 1) as i:
                    step(i)
                step(ITER - 1, last=(f == 3), late=True)

            def after(m, s):
                n = MIX_BASE[m] + s + RING
                rest(n, n % RING)

            def sigmoid(buf):
                own(v.tensor_scalar(buf, buf, 1.0, None, ALU.add))
                own(v.reciprocal(buf, buf))

            def y_rest(parts):
                for k0, k1, count in parts:
                    v.wait_ge(y_h, count)
                    v.tensor_tensor(y_lo[:, k0:k1, :], act[:, k0:k1, :], y_hi[:, k0:k1, :].bitcast(F32), ALU.subtract).then_inc(y_l, 1)

            def mixer_ab():
                def forget(p):
                    h = slice(2 * p, 2 * p + 2)
                    v.wait_ge(chunk_out, 2 * p + 2)
                    own(v.tensor_scalar(b_f[:, h, :], b_f[:, h, :], 0.5, 0.5, ALU.mult, ALU.add))
                    for a in (2 * p, 2 * p + 1):
                        v.tensor_scalar(b_f[:, a, :], b_f[:, a, :], oml[:, a:a + 1], lb[:, a:a + 1], ALU.mult, ALU.add).then_inc(dve, 1)
                    order[0] += 2
                    v.wait_ge(dve, order[0])
                    v.tensor_scalar(b_kc[:, h, :], b_f[:, h, :], -1.0, 1.0, ALU.mult, ALU.add).then_inc(f_ready, 1)

                def cumulate(p):
                    h = slice(2 * p, 2 * p + 2)
                    v.wait_ge(lf_ready, p + 1)
                    for a in (2 * p, 2 * p + 1):
                        ins = v.tensor_tensor_scan(b_b[:, a, :], const("reset"), b_lf[:, a, :], 0.0, ALU.mult, ALU.add)
                        ins.then_inc(dve, 1)
                    order[0] += 2
                    v.wait_ge(dve, order[0])
                    for a in (2 * p, 2 * p + 1):
                        bb = b_b[:, a, :].rearrange("p (c s) -> p c s", s=HGC)
                        ins = v.tensor_tensor(b_lf[:, a, :].rearrange("p (c s) -> p c s", s=HGC),
                                              bb[:, :, HGC - 1:HGC].broadcast_to([P, S // HGC, HGC]), bb, ALU.subtract)
                    ins.then_inc(b_ready, 1)

                def keys(p):
                    h = slice(2 * p, 2 * p + 2)
                    v.wait_ge(e_ready, p + 1)
                    own(v.tensor_tensor(b_kd[:, h, :], b_kc[:, h, :], b_b[:, h, :], ALU.mult))
                    v.tensor_tensor(b_kc[:, h, :], b_kc[:, h, :], b_lf[:, h, :], ALU.mult).then_inc(kd_ready, 1)

                def queries(p):
                    h = slice(2 * p, 2 * p + 2)
                    v.wait_ge(chunk_out, 10 + 2 * p)
                    v.tensor_tensor(b_q[:, h, :], b_q[:, h, :], b_eb[:, h, :], ALU.mult).then_inc(q_ready, 1)

                def states(t):
                    v.wait_ge(hg_ds, t + 1)
                    for c in range(4 * t, min(4 * t + 4, 7)):
                        for h in range(H):
                            src = acc[:, c % 4, h * P:(h + 1) * P]
                            if c == 0:
                                ins = v.tensor_copy(b_s[:, 0, h, :], src)
                            else:
                                ins = v.scalar_tensor_tensor(out=b_s[:, c, h, :], in0=b_s[:, c - 1, h, :],
                                                             scalar=b_eb[:, h, c * HGC + HGC - 1:c * HGC + HGC], in1=src, op0=ALU.mult, op1=ALU.add)
                            ins.then_inc(dve, 1)
                        order[0] += H
                        v.wait_ge(dve, order[0])
                    v.sem_inc(hg_s, 1)

                def heads():
                    for h in range(H):
                        v.wait_ge(hg_rs, h + 1)
                        own(v.scalar_tensor_tensor(out=b_o[:, h, :], in0=b_o[:, h, :], scalar=gain(C_HGN + h), in1=b_rs[:, h, :], op0=ALU.mult, op1=ALU.mult))
                        ins = v.tensor_tensor(act[:, h, :], b_o[:, h, :], b_g[:, h, :], ALU.mult)
                    ins.then_inc(y_f, 1)

                lower_bound()
                v.wait_ge(const_in, 16)
                after(0, -1)
                forget(0)
                after(0, 0)
                forget(1)
                after(0, 1)
                for p in range(2):
                    cumulate(p)
                after(0, 2)
                for p in range(2):
                    keys(p)
                after(0, 3)
                after(0, 4)
                queries(0)
                after(0, 5)
                queries(1)
                after(0, 6)
                for h in range(H):
                    v.wait_ge(hg_at, h + 1)
                    v.tensor_copy(b_kt[:, h, :, :], acc[:, h, 0:S].rearrange("p (t d) -> p t d", t=T))
                    v.tensor_tensor(b_at[:, h, :, :], acc[:, h, S:2 * S].rearrange("p (t d) -> p t d", t=T),
                                    const("bd").unsqueeze(1).broadcast_to([P, T, P]), ALU.mult).then_inc(hg_ev, 1)
                after(0, 7)
                states(0)
                after(0, 8)
                states(1)
                after(0, 9)
                own(v.memset(b_z[:, :, 0:2], 0.0))
                for p in range(2):
                    after(0, 10 + p)
                    h = slice(2 * p, 2 * p + 2)
                    v.wait_ge(chunk_out, 22 + 2 * p)
                    own(v.tensor_tensor(b_z[:, h, 2:S + 2], b_c[:, h, :], b_u[:, h, :], ALU.mult))
                    if p == 0:
                        heads()
                for w in (2, 1, 0):
                    for h in range(H):
                        if w == 2:
                            ins = v.tensor_scalar(b_c[:, h, :], b_z[:, h, 2:S + 2], gain(C_CW + 2 * H + h), gain(C_CB + h), ALU.mult, ALU.add)
                        else:
                            ins = v.scalar_tensor_tensor(out=b_c[:, h, :], in0=b_z[:, h, w:S + w], scalar=gain(C_CW + w * H + h), in1=b_c[:, h, :], op0=ALU.mult, op1=ALU.add)
                        ins.then_inc(dve, 1)
                    order[0] += H
                    v.wait_ge(dve, order[0])
                for p in range(2):
                    h = slice(2 * p, 2 * p + 2)
                    v.wait_ge(chunk_out, 26 + 2 * p)
                    v.tensor_tensor(act[:, 4 + 2 * p:6 + 2 * p, :], b_c[:, h, :], b_bg[:, h, :], ALU.mult).then_inc(y_f, 1)
                    y_rest(([(0, 4, 1), (4, 6, 2)], [(6, 8, 3)])[p])
                    after(0, 12 + p)
                for s in (14, 15):
                    after(0, s)

            def mixer_cd():
                after(1, -1)
                v.wait_ge(gt_mm, 1)
                v.wait_ge(fg_in, 64)
                v.tensor_scalar(row[:, 0, :], acc[0:H, 0, 0:S], gbias[:, 0:1], None, ALU.add)
                own(v.tensor_scalar(row[:, 1, :], acc[32:32 + H, 0, 0:S], gbias[:, 1:2], None, ALU.add))
                v.scalar_tensor_tensor(out=row[:, 2, :], in0=row[:, 1, :], scalar=-1.0, in1=row[:, 1, :], op0=ALU.mult, op1=ALU.min).then_inc(gt_na, 1)
                after(1, 0)
                after(1, 1)
                v.wait_ge(gt_ln, 1)
                own(v.scalar_tensor_tensor(out=row[:, 1, :], in0=row[:, 1, :], scalar=0.0, in1=row[:, 3, :], op0=ALU.min, op1=ALU.subtract))
                one_row = const("ones")[0:H, 0:1].broadcast_to([H, S])
                own(v.tensor_tensor_scan(row[:, 4, :], one_row, row[:, 1, :], 0.0, ALU.mult, ALU.add))
                own(v.tensor_tensor(row[:, 5, :], row[:, 0, :], row[:, 4, :], ALU.subtract))
                own(v.tensor_tensor_scan(row[:, 2, :], one_row, row[:, 5, :], 0.0, ALU.mult, ALU.max))
                own(v.tensor_scalar(row[:, 6, :], row[:, 2, :], -1.0, None, ALU.mult))
                v.tensor_tensor(row[:, 7, :], row[:, 6, :], row[:, 4, :], ALU.subtract).then_inc(gt_rows, 1)
                v.tensor_scalar(c_oe[:, :, :], c_oe[:, :, :], 0.5, 0.5, ALU.mult, ALU.add).then_inc(dve, 1)
                order[0] += 1
                after(1, 2)
                v.wait_ge(gt_tp, 1)
                v.tensor_copy(gcol, acc[:, 0, 0:2 * H]).then_inc(gt_col, 1)
                after(1, 3)
                for h in range(H):
                    v.wait_ge(gt_bc, h + 1)
                    v.tensor_tensor(c_dt[:, h, 0:S], acc[:, h, 0:S], const("m_ji")[:, 0:S], ALU.add)
                    v.tensor_tensor(c_dt[:, h, S:384], acc[:, h, P:S], const("m_ji")[:, S:384], ALU.add).then_inc(gt_pre, 1)
                for s in (4, 5, 6):
                    after(1, s)
                for h in range(H):
                    v.wait_ge(ml_s, h + 1)
                    v.wait_ge(gt_dt, h + 1)
                    v.tensor_tensor(c_dt[:, h, :], acc[:, h, 0:384], c_dt[:, h, :], ALU.mult).then_inc(ml_w, 1)
                for s in (7, 8):
                    after(1, s)
                for h in range(H):
                    v.wait_ge(ml_n, h + 1)
                    own(v.tensor_tensor(c_em[:, h, :], acc[:, h, S:2 * S], c_em[:, h, :], ALU.max))
                    own(v.scalar_tensor_tensor(out=c_em[:, h, :], in0=acc[:, h, S:2 * S], scalar=-1.0, in1=c_em[:, h, :], op0=ALU.mult, op1=ALU.max))
                    v.scalar_tensor_tensor(out=c_em[:, h, :], in0=c_em[:, h, :], scalar=EPS, in1=c_em[:, h, :], op0=ALU.mult, op1=ALU.mult).then_inc(ml_h, 1)
                after(1, 9)
                v.wait_ge(ml_h, H)
                for h in range(H):
                    v.wait_ge(ml_ss, h + 1)
                    v.scalar_tensor_tensor(out=c_rn[:, h, :], in0=acc[:, h, 0:S], scalar=1.0 / P, in1=c_em[:, h, :], op0=ALU.mult, op1=ALU.add).then_inc(ml_ar, 1)
                after(1, 10)
                for h in range(H):
                    v.wait_ge(ml_rs, h + 1)
                    own(v.scalar_tensor_tensor(out=c_h[:, h, :], in0=c_h[:, h, :], scalar=gain(C_MLN + h), in1=c_rn[:, h, :], op0=ALU.mult, op1=ALU.mult))
                    ins = v.tensor_tensor(act[:, h, :], c_h[:, h, :], c_oe[:, h, :], ALU.mult)
                    if h % 2:
                        ins.then_inc(y_f, 1)
                sin = const("sin").unsqueeze(1).broadcast_to([P, 2, S])

                def rotary(n, buf):
                    for half in range(2):
                        v.wait_ge(mb_rot, 2 * n + half + 1)
                        ins = v.tensor_tensor(c_rs[:, n, 512 * half:512 * half + 512].rearrange("p (h s) -> p h s", h=2),
                                              acc[:, 2 * n + half, :].rearrange("p (h s) -> p h s", h=2), sin, ALU.mult)
                        ins.then_inc(dve, 1)
                    order[0] += 2
                    v.wait_ge(dve, order[0])
                    v.wait_ge(mb_cos, n + 1)
                    v.tensor_tensor(buf[:, :, :], buf[:, :, :], c_rs[:, n, :].rearrange("p (h s) -> p h s", h=H), ALU.add).then_inc(mb_qk, 1)

                rotary(0, c_q)
                y_rest([(0, 2, 4)])
                after(1, 11)
                rotary(1, c_k)
                y_rest([(2, 4, 5)])
                after(1, 12)
                v.wait_ge(mb_qk, 2)
                for h in range(H):
                    v.wait_ge(mb_s, h + 1)
                    own(v.tensor_tensor(c_p[:, h, :], acc[:, h, 0:384], const("m_ij"), ALU.add))
                    v.tensor_reduce(nmax[:, 2 * h:2 * h + 1], c_p[:, h, 0:P], AX.X, ALU.max)
                    own(v.tensor_reduce(nmax[:, 2 * h + 1:2 * h + 2], c_p[:, h, P:384], AX.X, ALU.max))
                    v.tensor_scalar(nmax[:, 2 * h:2 * h + 2], nmax[:, 2 * h:2 * h + 2], -(P ** -0.5), None, ALU.mult).then_inc(mb_sm, 1)
                for h in range(H):
                    v.wait_ge(mb_p, h + 1)
                    own(v.reciprocal(rsum[:, 2 * h:2 * h + 2], rsum[:, 2 * h:2 * h + 2]))
                    v.tensor_scalar(c_p[:, h, 0:P], c_p[:, h, 0:P], rsum[:, 2 * h:2 * h + 1], None, ALU.mult)
                    v.tensor_scalar(c_p[:, h, P:384], c_p[:, h, P:384], rsum[:, 2 * h + 1:2 * h + 2], None, ALU.mult).then_inc(mb_pn, 1)
                after(1, 13)
                after(1, 14)
                y_rest([(4, 6, 6), (6, 8, 7)])
                after(1, 15)

            v.wait_ge(x_in, 16 * T)
            v.sem_inc(x_ready, 4)
            v.wait_ge(prow_t, 1)
            v.tensor_copy(pcol[:, :], ch[:, 2, 0:N_ROWS]).then_inc(pcol_done, 1)
            v.wait_ge(pcol_done, 1)

            def lower_bound():
                rows = pcol[:, C_LB:C_LB + 12].rearrange("p (r h) -> p r h", r=3)
                own(v.tensor_tensor(lbt, rows[:, 0, :], rows[:, 1, :], ALU.max))
                own(v.tensor_tensor(lbt, lbt, rows[:, 2, :], ALU.max))
                e = lbe.rearrange("p (r h) -> p r h", r=3)
                v.tensor_tensor(e, rows, lbt.unsqueeze(1).broadcast_to([P, 3, H]), ALU.subtract).then_inc(lb_sub, 1)
                v.wait_ge(lb_exp, 1)
                own(v.tensor_tensor(lbt, e[:, 0, :], e[:, 1, :], ALU.add))
                own(v.tensor_tensor(lbt, lbt, e[:, 2, :], ALU.add))
                own(v.reciprocal(lbt, lbt))
                own(v.tensor_tensor(lb, e[:, 0, :], lbt, ALU.mult))
                own(v.tensor_scalar(oml, lb, -1.0, 1.0, ALU.mult, ALU.add))

            scale = 1.0
            gains = [0, C_MIX, 8, 16, C_MIX + 8, 24]
            m = 0
            for kind, f in PHASES:
                norm(m, gains[m], scale)
                m += 1
                if kind == "ffn":
                    ffn(f)
                elif kind == "ab":
                    mixer_ab()
                else:
                    mixer_cd()
                scale = 0.5 if kind == "ffn" else 1.0
            for t in range(T):
                residual(6, scale, t)
            v.wait_ge(fg_in, 64)
            for t in range(T):
                v.wait_ge(rstd_ready, 2 * 6 + t + 1)
                v.wait_ge(x_ready, 4 * 6 + 2 * t + 2)
                own(v.tensor_scalar(xn[:, t, :], xs[:, t, :], rstd[:, t:t + 1], ROOT_D, ALU.mult, ALU.mult))
                v.tensor_tensor(xn[:, t, :], xn[:, t, :], fgain[:, :], ALU.mult).then_inc(y_out, 1)

        @block.tensor
        def _(pe):
            def three(dst, l_hi, l_lo, r_hi, r_lo, start, stop):
                pe.matmul(dst, l_hi, r_hi, start=start, stop=False, skip_group_check=True)
                pe.matmul(dst, l_hi, r_lo, start=False, stop=False, skip_group_check=True)
                return pe.matmul(dst, l_lo, r_hi, start=False, stop=stop, skip_group_check=True)

            def channels(dst, pos, j, first=None):
                c = slice(j * P, (j + 1) * P)
                for t in ((None,) if first is None else range(T)):
                    i = slice(0, S) if t is None else slice(t * P, (t + 1) * P)
                    if t is not None:
                        pe.wait_ge(xl_ready, 4 * first + 2 * t + 2)
                    for k in range(KD):
                        ins = three(dst[:, i], slot3(w_hi, pos)[:, k, c], slot3(w_lo, pos)[:, k, c], x_hi[:, k, i], x_lo[:, k, i], k == 0, k == KD - 1)
                return ins

            def tokens(dst, pos, t):
                c = slice(t * P, (t + 1) * P)
                for k in range(KD):
                    ins = three(dst, x_hi[:, k, c], x_lo[:, k, c], slot3(w_hi, pos)[:, k, :], slot3(w_lo, pos)[:, k, :], k == 0, k == KD - 1)
                return ins

            def project(pos, rows, start, done):
                for t in range(T):
                    c = slice(t * P, (t + 1) * P)
                    for r, k in rows:
                        for half in range(2):
                            w = slice(512 * half, 512 * half + 512)
                            ins = three(acc[:, 2 * t + half, :], y_hi[:, k, c], y_lo[:, k, c], slot2(w_hi, pos)[:, r, w], slot2(w_lo, pos)[:, r, w],
                                        start and r == 0, done and r == 1)
                    if done:
                        ins.then_inc(acc_done, 1)
                return ins

            def norm(m):
                for t in range(T):
                    pe.wait_ge(xn_ready, 2 * m + t + 1)
                    for half in range(2):
                        for k in range(4):
                            ins = pe.transpose(ch[:, 2 * t + half, k * P:(k + 1) * P], xn[:, t, (4 * half + k) * P:(4 * half + k + 1) * P], ident)
                        ins.then_inc(tp_ready, 1)

            def ffn(f, m):
                def step(i, last=False, first=None):
                    q0 = 2 * ITER * f + 2 * i
                    n0 = FFN_BASE[f] + 3 * i
                    for j in range(2):
                        if j == 0:
                            pe.wait_ge(lo_done, n0 + 1)
                        channels(ch[:, 2 * j, 0:S], 0, j, first if j == 0 else None).then_inc(gate_ready, 1)
                        if j == 0:
                            pe.wait_ge(lo_done, n0 + 2)
                        channels(ch[:, 2 * j + 1, 0:S], 1, j).then_inc(up_ready, 1)
                    pe.wait_ge(lo_done, n0 + 3)
                    for j in range(2):
                        pe.wait_ge(hid_lo, q0 + j + 1)
                        ins = project(2, [(j, j)], False, last and j == 1)
                    if not last:
                        ins.then_inc(out_used, 1)

                for b in range(4):
                    pe.matmul(acc[:, b, :], zb[:, 0:P], zb[:, :], start=True, stop=False, skip_group_check=True)
                step(0, first=m - 1)
                with pe.Fori(1, ITER - 1) as i:
                    step(i)
                step(ITER - 1, last=True)

            def slot(m, s, first=None):
                n = MIX_BASE[m] + s
                pe.wait_ge(lo_done, n + 1)
                for j in range(2):
                    c = 2 * s + j
                    if c >= 4:
                        pe.wait_ge(chunk_out, CHUNKS * m + c - 3)
                    dst = ch[:, c % 4, 0:S]
                    if s in TOK[m]:
                        ins = tokens(dst, n % RING, j)
                    else:
                        ins = channels(dst, n % RING, j, first if c == 0 else None)
                    ins.then_inc(chunk, 1)

            def out_slot(m, s, y_count):
                n = MIX_BASE[m] + 14 + s
                pe.wait_ge(lo_done, n + 1)
                pe.wait_ge(y_l, y_count)
                k0 = (AB_ROWS, CD_ROWS)[m][s]
                ins = project(n % RING, [(0, k0), (1, k0 + 1)], s == 0, s == 3)
                if s < 3:
                    ins.then_inc(out_used, 1)

            def mixer_ab():
                for s in range(7):
                    slot(0, s, 1)
                pe.wait_ge(kd_ready, 2)
                pe.wait_ge(q_ready, 2)
                for h in range(H):
                    for t in range(T):
                        pe.transpose(acc[:, h, t * P:(t + 1) * P], b_kc[:, h, t * P:(t + 1) * P], ident)
                    for t in range(T):
                        c = slice(t * P, (t + 1) * P)
                        ins = pe.matmul(acc[:, h, S + t * P:S + (t + 1) * P], b_kd[:, h, c], b_q[:, h, c], start=True, stop=True)
                    ins.then_inc(hg_at, 1)
                slot(0, 7)
                pe.wait_ge(hg_ev, H)
                pe.wait_ge(chunk_out, 8)
                for t in range(T):
                    if t:
                        slot(0, 8)
                        pe.wait_ge(hg_s, 1)
                    for c in range(4 if t == 0 else 3):
                        r = slice(HGC * c, HGC * (c + 1))
                        for h in range(H):
                            ins = pe.matmul(acc[:, c, h * P:(h + 1) * P], b_kt[r, h, t, :], b_v[r, t, h * P:(h + 1) * P], start=True, stop=True)
                    ins.then_inc(hg_ds, 1)
                slot(0, 9)
                pe.wait_ge(hg_s, 2)
                for h in range(H):
                    for t in range(T):
                        pe.matmul(acc[:, h, t * P:(t + 1) * P], b_v[:, t, h * P:(h + 1) * P], b_at[:, h, t, :], start=True, stop=False, skip_group_check=True)
                        for c in range(max(4 * t, 1), 4 * t + 4):
                            s = slice(c * HGC, (c + 1) * HGC)
                            ins = pe.matmul(acc[:, h, s], b_s[:, c - 1, h, :], b_q[:, h, s], start=False, stop=(c == 4 * t + 3), skip_group_check=True)
                    ins.then_inc(hg_o, 1)
                slot(0, 10)
                for h in range(H):
                    pe.wait_ge(hg_oc, h + 1)
                    pe.matmul(acc[:, h, 0:S], ones, b_sq[:, h, :], start=True, stop=True).then_inc(hg_ss, 1)
                for s in (11, 12, 13):
                    slot(0, s)
                pe.wait_ge(hg_rs, H)
                for s, count in enumerate((1, 1, 2, 3)):
                    out_slot(0, s, count)

            def mixer_cd():
                slot(1, 0, 4)
                pe.wait_ge(fg_in, 64)
                for k in range(KD):
                    ins = pe.matmul(acc[0:36, 0, 0:S], wgate[:, k, :], act[:, k, :], start=(k == 0), stop=(k == KD - 1))
                ins.then_inc(gt_mm, 1)
                slot(1, 1)
                slot(1, 2)
                pe.wait_ge(gt_rows, 1)
                for t in range(T):
                    ins = pe.transpose(acc[:, 0, t * H:(t + 1) * H], row[:, 5, t * P:(t + 1) * P], ident[0:H, 0:H])
                ins.then_inc(gt_tp, 1)
                slot(1, 3)
                pe.wait_ge(gt_col, 1)
                sel = const("sel").rearrange("p (h m) -> p h m", h=H)
                for h in range(H):
                    pe.matmul(acc[:, h, :], sel[0:H, h, :], row[:, 6:8, :].rearrange("p n s -> p (n s)"), start=True, stop=True).then_inc(gt_bc, 1)
                for s in (4, 5, 6):
                    slot(1, s)
                pe.wait_ge(gt_dt, H)
                pe.wait_ge(chunk_out, CHUNKS + 12)
                for h in range(H):
                    pe.matmul(acc[:, h, 0:S], c_lk[:, h, 0:P], c_lq[:, h, :], start=True, stop=True)
                    pe.matmul(acc[:, h, S:384], c_lk[:, h, P:S], c_lq[:, h, P:S], start=True, stop=True).then_inc(ml_s, 1)
                slot(1, 7)
                slot(1, 8)
                pe.wait_ge(chunk_out, CHUNKS + 16)
                for h in range(H):
                    pe.wait_ge(ml_w, h + 1)
                    g = slice(h * P, (h + 1) * P)
                    for lhs, at in (((c_lv[:, 0, g], c_lv[:, 1, g]), 0), ((ones, ones), S)):
                        pe.matmul(acc[:, h, at:at + S], lhs[0], c_dt[:, h, 0:S], start=True, stop=False, skip_group_check=True)
                        ins = pe.matmul(acc[:, h, at + P:at + S], lhs[1], c_dt[:, h, S:384], start=False, stop=True, skip_group_check=True)
                    ins.then_inc(ml_n, 1)
                slot(1, 9)
                for h in range(H):
                    pe.wait_ge(ml_sq, h + 1)
                    pe.matmul(acc[:, h, 0:S], ones, c_sq[:, h, :], start=True, stop=True).then_inc(ml_ss, 1)
                slot(1, 10)

                def rotate(n, buf, moved):
                    for half in range(2):
                        pe.wait_ge(chunk_out, CHUNKS + moved + 2 * half)
                        pe.matmul(acc[:, 2 * n + half, :], const("rot"), buf[:, 2 * half:2 * half + 2, :].rearrange("p h s -> p (h s)"),
                                  start=True, stop=True).then_inc(mb_rot, 1)

                pe.wait_ge(ml_ar, H)
                rotate(0, c_q, 18)
                slot(1, 11)
                rotate(1, c_k, 22)
                slot(1, 12)
                pe.wait_ge(mb_qk, 2)
                for h in range(H):
                    pe.matmul(acc[:, h, 0:P], c_q[:, h, 0:P], c_k[:, h, 0:P], start=True, stop=True)
                    pe.matmul(acc[:, h, P:384], c_q[:, h, P:S], c_k[:, h, :], start=True, stop=True).then_inc(mb_s, 1)
                slot(1, 13)
                pe.wait_ge(mb_sm, H)
                pe.wait_ge(chunk_out, 2 * CHUNKS)
                for h in range(H):
                    pe.wait_ge(mb_pn, h + 1)
                    for b in range(3):
                        ins = pe.transpose(ch[:, h, b * P:(b + 1) * P], c_p[:, h, b * P:(b + 1) * P], ident)
                    ins.then_inc(mb_pt, 1)
                out_slot(1, 0, 4)
                for h in range(H):
                    pe.wait_ge(mb_ptc, h + 1)
                    g = slice(h * P, (h + 1) * P)
                    pe.matmul(ch[:, h, 0:S], c_v[:, 0, g], c_pt[:, h, 0:S], start=True, stop=False, skip_group_check=True)
                    pe.matmul(ch[:, h, P:S], c_v[:, 1, g], c_pt[:, h, S:384], start=False, stop=True, skip_group_check=True).then_inc(mb_o, 1)
                for s, count in ((1, 5), (2, 6), (3, 7)):
                    out_slot(1, s, count)

            pe.wait_ge(ident_in, 16)
            pe.wait_ge(small_in, 7 * 16)
            pe.wait_ge(setup, 5)
            pe.transpose(ch[:, 2, 0:N_ROWS], prow[0:N_ROWS, :], ident[0:N_ROWS, 0:N_ROWS]).then_inc(prow_t, 1)
            pe.wait_ge(pcol_done, 1)
            m = 0
            for kind, f in PHASES:
                norm(m)
                if kind == "ffn":
                    if m:
                        pe.wait_ge(x_ready, 4 * m + 4)
                m += 1
                if kind == "ffn":
                    ffn(f, m)
                elif kind == "ab":
                    pe.wait_ge(const_in, 16)
                    mixer_ab()
                else:
                    mixer_cd()


_INS = ["x", "ffn_norm", "ffn_w_in", "ffn_w_out", "mix_norm", "ab_w_in", "ab_w_out", "hgrn_lb_logits", "hgrn_out_norm",
        "conv_w", "conv_b", "cd_w_in", "cd_w_out", "mlstm_gate_bias", "mlstm_out_norm", "final_norm"]


def kernel(**inputs):
    import concourse.bacc as bacc
    from concourse.bass_utils import run_bass_kernel_spmd

    nc = bacc.Bacc("TRN2", target_bir_lowering=False, num_devices=1)
    arrays = {f"in_{n}": np.ascontiguousarray(inputs[n]) for n in _INS}
    arrays["in_consts"] = shape_constants()
    args = [nc.dram_tensor(n, a.shape, mybir.dt.from_np(a.dtype), kind="ExternalInput").ap() for n, a in arrays.items()]
    args.append(nc.dram_tensor("out_0", (1, S, D), F32, kind="ExternalOutput").ap())
    build(nc, *args)
    r = run_bass_kernel_spmd(nc, [arrays], core_ids=[0])
    return r.results[0]["out_0"]
```

```python
from contextlib import ExitStack

import numpy as np

import concourse.bass as bass
from concourse import mybir

F32 = mybir.dt.float32
F32R = mybir.dt.float32r
BF16 = mybir.dt.bfloat16
ALU = mybir.AluOpType
ACT = mybir.ActivationFunctionType
AX = mybir.AxisListType

P = 128
D = 1024
S = 256
T = S // P
KD = D // P
F = 2816
G = 512
H = G // P
PAIR = 2 * P
SLOT = KD * PAIR
ITER = F // PAIR
RING = 3
NMIX = 18
HGC = 32
EPS = 1e-6
MEAN = D ** -0.5
MASKED = -1e30

FFN_BASE = [0, 3 * ITER + NMIX, 6 * ITER + NMIX, 9 * ITER + 2 * NMIX]
MIX_BASE = [3 * ITER, 9 * ITER + NMIX]
OUT_FFN = [0, ITER + 2, 2 * ITER + 1, 3 * ITER + 3]
OUT_MIX = [ITER - 1, 3 * ITER]
PHASES = [("ffn", 0), ("ab", 0), ("ffn", 1), ("ffn", 2), ("cd", 1), ("ffn", 3)]
FIRST_SLOT = [(FFN_BASE if kind == "ffn" else MIX_BASE)[f] for kind, f in PHASES]
CHUNKS = 28

C_HGN, C_CW, C_CB, C_MLN, C_LB, N_ROWS = 0, 4, 16, 20, 24, 36

CONST = dict(ident=128, ones=128, m_ij=384, m_ji=384, bd=128, reset=256, cos=256, sin=256, rot=128, sel=512)
C_AT = {}
for _n, _w in CONST.items():
    C_AT[_n] = sum(CONST[m] for m in list(CONST)[:list(CONST).index(_n)])
N_CONST = sum(CONST.values())


def shape_constants():
    a = np.arange(P)
    c = {}
    c["ident"] = np.eye(P)
    c["ones"] = np.ones((P, P))
    low = np.where(a[None, :] <= a[:, None], 0.0, MASKED)
    zero = np.zeros((P, P))
    c["m_ij"] = np.concatenate([low, zero, low], 1)
    c["m_ji"] = np.concatenate([low.T, zero, low.T], 1)
    c["bd"] = ((a[:, None] // HGC == a[None, :] // HGC) & (a[:, None] <= a[None, :])).astype(float)
    c["reset"] = np.tile((np.arange(S) % HGC != 0).astype(float), (P, 1))
    half = P // 4 // 2
    inv = np.float32(500000.0) ** (-np.arange(half, dtype=np.float32) * np.float32(2.0) / np.float32(2 * half))
    ang = np.arange(S, dtype=np.float32)[None, :] * inv[:, None].astype(np.float32)
    c["cos"] = np.concatenate([np.cos(ang), np.cos(ang), np.ones((P - 2 * half, S))], 0)
    c["sin"] = np.concatenate([np.sin(ang), np.sin(ang), np.zeros((P - 2 * half, S))], 0)
    rot = np.zeros((P, P))
    for d in range(half):
        rot[d + half, d] = -1.0
        rot[d, d + half] = 1.0
    c["rot"] = rot
    sel = np.zeros((P, H, P))
    for h in range(H):
        sel[h, h, :] = 1.0
    c["sel"] = sel.reshape(P, H * P)
    return np.ascontiguousarray(np.concatenate([c[n] for n in CONST], 1).astype(np.float32))


def build(nc, x, ffn_norm, ffn_w_in, ffn_w_out, mix_norm, ab_w_in, ab_w_out, hgrn_lb_logits, hgrn_out_norm,
          conv_w, conv_b, cd_w_in, cd_w_out, mlstm_gate_bias, mlstm_out_norm, final_norm, consts, out):
    ctx = ExitStack()
    with ctx:
        def sb(name, shape, dt=F32):
            return ctx.enter_context(nc.sbuf_tensor(name, shape, dt))

        def sem(name):
            return ctx.enter_context(nc.semaphore(name))

        raw = sb("raw", [P, RING, SLOT])
        w_hi = sb("w_hi", [P, RING, SLOT], F32R)
        w_lo = sb("w_lo", [P, RING, SLOT], F32R)
        xs = sb("xs", [P, T, D])
        xn = sb("xn", [P, T, D])
        act = sb("act", [P, KD, S])
        x_hi = sb("x_hi", [P, KD, S], F32R)
        x_lo = sb("x_lo", [P, KD, S], F32R)
        y_hi = sb("y_hi", [P, KD, S], F32R)
        y_lo = sb("y_lo", [P, KD, S], F32R)
        mix = sb("mix", [P, 15, H * S])
        cst = sb("cst", [P, N_CONST])
        prow = sb("prow", [P, P])
        pcol = sb("pcol", [P, N_ROWS])
        gains = sb("gains", [P, D])
        gbias = sb("gbias", [H, 2])
        wgate = sb("wgate", [P, KD, 36])
        zb = sb("zb", [P, 512], BF16)
        col = sb("col", [P, 64])

        ch = ctx.enter_context(nc.psum_tensor("ch", [P, 4, 512], F32))
        acc = ctx.enter_context(nc.psum_tensor("acc", [P, 4, 512], F32))

        def const(name):
            return cst[:, C_AT[name]:C_AT[name] + CONST[name]]

        ident, ones = const("ident"), const("ones")
        eps_c, one_c = col[:, 0:1], col[:, 1:2]
        half_c, ssq, msum, rstd = col[:, 63:64], col[:, 2:6], col[:, 6:8], col[:, 56:58]
        lb, oml = col[:, 8:12], col[:, 12:16]
        lbt, lbe = col[:, 16:20], col[:, 20:32]
        gcol = col[:, 32:40]
        nmax, rsum = col[:, 40:48], col[:, 48:56]

        def gain(at):
            return pcol[:, at:at + 1]

        def m4(n):
            return mix[:, n, :].rearrange("p (h s) -> p h s", h=H)

        f_sig = mix[:, 1, 0:2 * S].rearrange("p (j s) -> p j s", j=2)
        b_f, b_lf, b_b, b_eb, b_kc, b_kd = (m4(n) for n in range(6))
        b_q = m4(7)
        b_kt = mix[:, 0, :].rearrange("p (h t d) -> p h t d", h=H, t=T)
        b_at = mix[:, 1, :].rearrange("p (h t d) -> p h t d", h=H, t=T)
        b_v = mix[:, 8, :].rearrange("p (t c) -> p t c", t=T)
        b_s = mix[:, 9:13, :].rearrange("p n c -> p (n c)")[:, 0:7 * G].rearrange("p (c h v) -> p c h v", c=7, h=H)
        b_g = m4(13)
        b_c, b_z = m4(14), mix[:, 2:4, :].rearrange("p n c -> p (n c)")[:, 0:H * (S + 2)].rearrange("p (h s) -> p h s", h=H)
        b_o, b_sq = xn[:, 0, :].rearrange("p (h s) -> p h s", h=H), xn[:, 1, :].rearrange("p (h s) -> p h s", h=H)
        b_u, b_bg, b_rs = m4(5), m4(4), m4(7)
        c_q, c_k, c_lk, c_lq = m4(0), m4(1), m4(3), m4(4)
        c_v = mix[:, 2, :].rearrange("p (t c) -> p t c", t=T)
        c_lv = mix[:, 5, :].rearrange("p (t c) -> p t c", t=T)
        c_dt = mix[:, 6:8, :].rearrange("p n c -> p (n c)")[:, 0:H * 384].rearrange("p (h c) -> p h c", h=H)
        c_em = m4(8)
        c_p = mix[:, 9:11, :].rearrange("p n c -> p (n c)")[:, 0:H * 384].rearrange("p (h c) -> p h c", h=H)
        c_rs = mix[:, 9:11, :]
        c_pt = mix[:, 11:13, :].rearrange("p n c -> p (n c)")[:, 0:H * 384].rearrange("p (h c) -> p h c", h=H)
        c_oe, c_h, c_sq = m4(13), m4(14), m4(9)
        c_rn = m4(11)
        row = mix[0:H, 11:13, :].rearrange("p n c -> p (n c)").rearrange("p (n s) -> p n s", s=S)

        slot_in = [sem(f"slot_in{r}") for r in range(RING)]
        hi_done = sem("hi_done")
        lo_done = sem("lo_done")
        out_used = sem("out_used")
        ident_in = sem("ident_in")
        small_in = sem("small_in")
        x_in = [sem(f"x_in{t}") for t in range(T)]
        const_in = sem("const_in")
        gate_in = sem("gate_in")
        gains_in = sem("gains_in")
        setup = sem("setup")
        prow_t = sem("prow_t")
        lb_sub = sem("lb_sub")
        lb_exp = sem("lb_exp")
        dve = sem("dve_order")
        actq = sem("act_order")
        pool_order = sem("pool_order")
        x_ready = sem("x_ready")
        ssq_ready = sem("ssq_ready")
        rstd_ready = sem("rstd_ready")
        xn_ready = sem("xn_ready")
        tp_ready = sem("tp_ready")
        xh_ready = sem("xh_ready")
        xl_ready = sem("xl_ready")
        xt_ready = sem("xt_ready")
        gate_ready = sem("gate_ready")
        up_ready = sem("up_ready")
        gate_silu = sem("gate_silu")
        hid = sem("hid")
        hid_hi = sem("hid_hi")
        hid_lo = sem("hid_lo")
        acc_done = sem("acc_done")
        chunk = sem("chunk")
        chunk_out = sem("chunk_out")
        y_f = sem("y_f")
        y_h = sem("y_h")
        y_l = sem("y_l")
        f_ready = sem("f_ready")
        lf_ready = sem("lf_ready")
        b_ready = sem("b_ready")
        e_ready = sem("e_ready")
        kd_ready = sem("kd_ready")
        q_ready = sem("q_ready")
        hg_at = sem("hg_at")
        hg_ev = sem("hg_ev")
        hg_ds = sem("hg_ds")
        hg_s = sem("hg_s")
        hg_o = sem("hg_o")
        hg_oc = sem("hg_oc")
        hg_ss = sem("hg_ss")
        hg_rs = sem("hg_rs")
        gt_mm = sem("gt_mm")
        gt_na = sem("gt_na")
        gt_ln = sem("gt_ln")
        gt_rows = sem("gt_rows")
        gt_tp = sem("gt_tp")
        gt_col = sem("gt_col")
        gt_bc = sem("gt_bc")
        gt_pre = sem("gt_pre")
        gt_dt = sem("gt_dt")
        ml_s = sem("ml_s")
        ml_w = sem("ml_w")
        ml_n = sem("ml_n")
        ml_h = sem("ml_h")
        ml_sq = sem("ml_sq")
        ml_ss = sem("ml_ss")
        ml_ar = sem("ml_ar")
        ml_rs = sem("ml_rs")
        mb_rot = sem("mb_rot")
        mb_cos = sem("mb_cos")
        mb_qk = sem("mb_qk")
        mb_s = sem("mb_s")
        mb_sm = sem("mb_sm")
        mb_p = sem("mb_p")
        mb_pn = sem("mb_pn")
        mb_pt = sem("mb_pt")
        mb_ptc = sem("mb_ptc")
        mb_o = sem("mb_o")
        out_done = sem("out_done")

        def slot3(t, r):
            return t[:, r, :].rearrange("p (k n) -> p k n", k=KD)

        def slot2(t, r):
            return t[:, r, :].rearrange("p (r n) -> p r n", r=2)

        AB_COLS = [(1, 0), (1, 1), (2, 0), (2, 1), (0, 0), (0, 1), (3, 0), (3, 1), (5, 0), (5, 1), (6, 0), (6, 1), (4, 0), (4, 1)]
        CD_COLS = [(3, 0), (3, 1), (0, 0), (0, 1), (1, 0), (1, 1), (2, 0), (2, 1), (4, 0), (4, 1), (5, 0), (5, 1), (6, 0), (6, 1)]
        AB_ROWS, CD_ROWS = [0, 2, 4, 6], [0, 2, 4, 6]
        TOK = (2, 3), (6, 7, 12, 13)

        NORMS = [ffn_norm[0, 0], mix_norm[0], ffn_norm[0, 1], ffn_norm[1, 0], mix_norm[1], ffn_norm[1, 1], final_norm]

        def gain_rows(m):
            return NORMS[m].rearrange("(a n) -> a n", a=1).broadcast_to([P, D])

        block = ctx.enter_context(nc.Block())

        @block.sync
        def _(sp):
            for t in range(T):
                sp.dma_start(xs[:, t, :], x[0, t * P:(t + 1) * P, :]).then_inc(x_in[t], 16)

            def load(pos, n, dst, src, first=False):
                if not first:
                    sp.wait_ge(lo_done, n - (RING - 1))
                sp.dma_start(dst, src).then_inc(slot_in[pos], 16)

            def ffn(f):
                win, wout = ffn_w_in[f // 2, f % 2], ffn_w_out[f // 2, f % 2]

                def step(i, first=False):
                    n = FFN_BASE[f] + 3 * i
                    for kind in range(2):
                        load(kind, n + kind, slot3(raw, kind),
                             win[:, bass.ds(kind * F + i * PAIR, PAIR)].rearrange("(k p) n -> p k n", p=P), first)
                    load(2, n + 2, slot2(raw, 2),
                         wout[bass.ds(i * PAIR, PAIR), :].rearrange("(r p) n -> p r n", p=P), first)

                if f == 0:
                    step(0, True)
                    sp.dma_start(cst[:, P:N_CONST], consts[:, P:N_CONST]).then_inc(const_in, 16)
                with sp.Fori(1 if f == 0 else 0, ITER) as i:
                    step(i)

            def mixer(m):
                win, wout = (ab_w_in, cd_w_in)[m][0], (ab_w_out, cd_w_out)[m][0]
                for s in range(14):
                    g, half = (AB_COLS, CD_COLS)[m][s]
                    c0 = g * G + half * PAIR + (2 * H if m == 1 and g >= 4 else 0)
                    n = MIX_BASE[m] + s
                    load(n % RING, n, slot3(raw, n % RING), win[:, c0:c0 + PAIR].rearrange("(k p) n -> p k n", p=P))
                for s in range(4):
                    r0 = (AB_ROWS, CD_ROWS)[m][s] * P
                    n = MIX_BASE[m] + 14 + s
                    load(n % RING, n, slot2(raw, n % RING), wout[r0:r0 + PAIR, :].rearrange("(r p) n -> p r n", p=P))

            for kind, f in PHASES:
                if kind == "ffn":
                    ffn(f)
                else:
                    mixer(f)
            for t in range(T):
                for half in range(2):
                    c = slice(512 * half, 512 * half + 512)
                    sp.wait_ge(xn_ready, 4 * 6 + 2 * t + half + 1)
                    sp.dma_start(out[0, t * P:(t + 1) * P, c], xn[:, t, c]).then_inc(out_done, 16)
            sp.wait_ge(out_done, 16 * 2 * T)

        @block.gpsimd
        def _(pool):
            pool.memset(zb[:, :], 0.0).then_inc(setup, 1)
            pool.memset(eps_c, EPS).then_inc(setup, 1)
            pool.memset(one_c, 1.0).then_inc(setup, 1)
            pool.memset(half_c, -0.5).then_inc(setup, 1)
            pool.memset(wgate[:, :, :], 0.0).then_inc(setup, 1)
            pool.wait_ge(setup, 5)
            with nc.allow_non_contiguous_dma(reason="eight columns of gate weights, eight biases"):
                for j in range(2):
                    pool.dma_start(wgate[:, :, 32 * j:32 * j + H],
                                   cd_w_in[0][:, 4 * G + H * j:4 * G + H * j + H].rearrange("(k p) n -> p k n", p=P)).then_inc(gate_in, 16)
                pool.dma_start(gbias[:, :], mlstm_gate_bias[0].rearrange("j h -> h j")).then_inc(gate_in, 16)
            for m in range(7):
                for t in range(T):
                    n = 2 * m + t
                    pool.wait_ge(ssq_ready, n + 1)
                    pool.tensor_scalar(msum[:, t:t + 1], ssq[:, 2 * t:2 * t + 1], ssq[:, 2 * t + 1:2 * t + 2], EPS, ALU.add, ALU.add).then_inc(pool_order, 1)
                    pool.wait_ge(pool_order, n + 1)
                    pool.tensor_tensor(rstd[:, t:t + 1], msum[:, t:t + 1], half_c, ALU.pow).then_inc(rstd_ready, 1)
                if m == 4:
                    pool.wait_ge(xl_ready, 4 * m + 4)
                    pool.tensor_tensor(act[:, :, :], x_hi[:, :, :].bitcast(F32), x_lo[:, :, :].bitcast(F32), ALU.add).then_inc(xt_ready, 1)
                    pool.wait_ge(const_in, 16)
                    cos = const("cos").unsqueeze(1).broadcast_to([P, H, S])
                    for n, buf in enumerate((c_q, c_k)):
                        pool.wait_ge(mb_rot, 2 * n + 2)
                        pool.tensor_tensor(buf[:, :, :], buf[:, :, :], cos, ALU.mult).then_inc(mb_cos, 1)

        @block.scalar
        def _(ae):
            def loads():
                ae.dma_start(gains[:, :], gain_rows(0)).then_inc(gains_in, 16)
                ae.dma_start(cst[:, 0:P], consts[:, 0:P]).then_inc(ident_in, 16)

            def small_loads():
                for at, src in ((C_HGN, hgrn_out_norm[0]),
                                (C_CW, conv_w[0].rearrange("w (h p) -> (w h) p", p=P)),
                                (C_CB, conv_b[0].rearrange("(h p) -> h p", p=P)),
                                (C_MLN, mlstm_out_norm[0]),
                                (C_LB, hgrn_lb_logits.rearrange("r (h p) -> (r h) p", p=P))):
                    ae.dma_start(prow[at:at + src.shape[0], :], src).then_inc(small_in, 16)

            order = [0]

            def own(ins):
                order[0] += 1
                ins.then_inc(actq, 1)
                ae.wait_ge(actq, order[0])

            def round_slot(pos, landed):
                ae.wait_ge(slot_in[pos], landed)
                ae.activation(w_hi[:, pos, :], raw[:, pos, :], ACT.Copy).then_inc(hi_done, 1)

            def split_out(f, i):
                n = FFN_BASE[f] + 2
                ae.wait_ge(out_used, OUT_FFN[f] + i)
                round_slot(n % RING, 16 * (n // RING + 1) + 16 * i)

            def split_in(f, i, kind):
                n = FFN_BASE[f] + RING + kind
                ae.wait_ge((gate_ready, up_ready)[kind], 2 * ITER * f + 2 * i + 2)
                round_slot(n % RING, 16 * (n // RING + 1) + 16 * i)

            def norm(m):
                for t in range(T):
                    for half in range(2):
                        ae.wait_ge(x_ready, 4 * m + 2 * t + half + 1)
                        c = slice(512 * half, 512 * half + 512)
                        ins = ae.activation(xn[:, t, c], xs[:, t, c], ACT.Square, scale=MEAN, accum_out=ssq[:, 2 * t + half:2 * t + half + 1])
                    ins.then_inc(ssq_ready, 1)
                if m == 6:
                    return
                for b in range(4):
                    t, half = b // 2, b % 2
                    sl = (slice(None), slice(4 * half, 4 * half + 4), slice(t * P, (t + 1) * P))
                    ae.wait_ge(tp_ready, 4 * m + b + 1)
                    ae.activation(x_hi[sl], ch[:, b, :].rearrange("p (k s) -> p k s", k=4), ACT.Copy).then_inc(xh_ready, 1)
                ae.wait_ge(xn_ready, 4 * m + 4)
                ae.dma_start(gains[:, :], gain_rows(m + 1)).then_inc(gains_in, 16)

            def ffn(f):
                def step(i, last=False, f_first=False):
                    q0 = 2 * ITER * f + 2 * i

                    def hidden(j):
                        ae.wait_ge(hid, q0 + j + 1)
                        ae.activation(y_hi[:, j, :], act[:, j, :], ACT.Copy).then_inc(hid_hi, 1)

                    if not f_first:
                        split_out(f, i)
                    for j in range(2):
                        ae.wait_ge(gate_ready, q0 + j + 1)
                        ae.activation(f_sig[:, j, :], ch[:, 2 * j, 0:S], ACT.Silu).then_inc(gate_silu, 1)
                        if j == 0:
                            hidden(0)
                    if not last:
                        split_in(f, i, 0)
                    hidden(1)
                    if not last:
                        split_in(f, i, 1)

                if f == 0:
                    step(0, f_first=True)
                with ae.Fori(1 if f == 0 else 0, ITER - 1 if f == 3 else ITER) as i:
                    step(i)
                if f == 3:
                    step(ITER - 1, last=True)

            def after(m, s):
                if s < 0:
                    ae.wait_ge(out_used, OUT_MIX[m])
                elif s < 14:
                    ae.wait_ge(chunk, CHUNKS * m + 2 * s + 2)
                else:
                    ae.wait_ge(out_used, OUT_MIX[m] + s - 13)
                n = MIX_BASE[m] + s + RING
                round_slot(n % RING, 16 * (n // RING + 1))

            def chunks(m, s, *moves):
                for j in range(2):
                    c = 2 * s + j
                    ae.wait_ge(chunk, CHUNKS * m + c + 1)
                    src = ch[:, c % 4, 0:S]
                    for k, (dst, func, scale) in enumerate(moves):
                        ins = ae.activation(dst(j), src, func, scale=scale)
                    ins.then_inc(chunk_out, 1)
                after(m, s)

            def y_split(parts):
                for k0, k1, count in parts:
                    ae.wait_ge(y_f, count)
                    ae.activation(y_hi[:, k0:k1, :], act[:, k0:k1, :], ACT.Copy).then_inc(y_h, 1)

            def mixer_ab():
                after(0, -1)
                ae.preload_act_table_set("natural_log_exp_and_others")
                ae.wait_ge(lb_sub, 1)
                ae.activation(lbe, lbe, ACT.Exp).then_inc(lb_exp, 1)
                ae.preload_act_table_set("silu_and_others")
                for s in (0, 1):
                    chunks(0, s, (lambda j: b_f[:, 2 * s + j, :], ACT.Tanh, 0.5))
                ae.preload_act_table_set("natural_log_exp_and_others")
                for p in range(2):
                    ae.wait_ge(f_ready, p + 1)
                    ae.activation(b_lf[:, 2 * p:2 * p + 2, :], b_f[:, 2 * p:2 * p + 2, :], ACT.Ln).then_inc(lf_ready, 1)
                chunks(0, 2, (lambda j: b_v[:, j, 0:PAIR], ACT.Copy, 1.0))
                for p in range(2):
                    h = slice(2 * p, 2 * p + 2)
                    ae.wait_ge(b_ready, p + 1)
                    ae.activation(b_lf[:, h, :], b_lf[:, h, :], ACT.Exp)
                    own(ae.activation(b_eb[:, h, :], b_b[:, h, :], ACT.Exp))
                    ae.activation(b_b[:, h, :], b_b[:, h, :], ACT.Exp, scale=-1.0).then_inc(e_ready, 1)
                chunks(0, 3, (lambda j: b_v[:, j, PAIR:2 * PAIR], ACT.Copy, 1.0))
                ae.preload_act_table_set("silu_and_others")
                for s in (4, 5):
                    chunks(0, s, (lambda j: b_q[:, 2 * s - 8 + j, :], ACT.Silu, 1.0))
                for s in (6, 7):
                    chunks(0, s, (lambda j: b_g[:, 2 * s - 12 + j, :], ACT.Silu, 1.0))
                ae.preload_act_table_set("natural_log_exp_and_others")
                for s in (8, 9):
                    chunks(0, s, (lambda j: b_c[:, 2 * s - 16 + j, :], ACT.Copy, 1.0))
                for h in range(H):
                    ae.wait_ge(hg_o, h + 1)
                    ae.activation(b_o[:, h, :], acc[:, h, 0:S], ACT.Copy)
                    ae.activation(b_sq[:, h, :], acc[:, h, 0:S], ACT.Square).then_inc(hg_oc, 1)
                chunks(0, 10, (lambda j: b_u[:, j, :], ACT.Copy, 1.0))
                for h in range(H):
                    ae.wait_ge(hg_ss, h + 1)
                    own(ae.activation(b_rs[:, h, :], acc[:, h, 0:S], ACT.Ln, bias=eps_c, scale=1.0 / P))
                    ae.activation(b_rs[:, h, :], b_rs[:, h, :], ACT.Exp, scale=-0.5).then_inc(hg_rs, 1)
                ae.preload_act_table_set("silu_and_others")
                chunks(0, 11, (lambda j: b_u[:, 2 + j, :], ACT.Copy, 1.0))
                y_split([(0, 4, 1)])
                for s in (12, 13):
                    chunks(0, s, (lambda j: b_bg[:, 2 * s - 24 + j, :], ACT.Copy, 1.0))
                    y_split([(2 * s - 20, 2 * s - 18, s - 10)])
                for s in (14, 15, 16):
                    after(0, s)

            def mixer_cd():
                after(1, -1)
                for s in (0, 1):
                    chunks(1, s, (lambda j: c_oe[:, 2 * s + j, :], ACT.Tanh, 0.5))
                ae.preload_act_table_set("natural_log_exp_and_others")
                ae.wait_ge(gt_na, 1)
                own(ae.activation(row[:, 2, :], row[:, 2, :], ACT.Exp))
                ae.activation(row[:, 3, :], row[:, 2, :], ACT.Ln, bias=one_c[0:H, :]).then_inc(gt_ln, 1)
                for s in (2, 3):
                    chunks(1, s, (lambda j: c_lq[:, 2 * s - 4 + j, :], ACT.Copy, P ** -0.5))
                chunks(1, 4, (lambda j: c_lk[:, j, :], ACT.Copy, 1.0))
                for h in range(H):
                    ae.wait_ge(gt_pre, h + 1)
                    ae.activation(c_em[:, h, :], acc[:, h, S:2 * S], ACT.Exp)
                    ae.activation(c_dt[:, h, 0:S], c_dt[:, h, 0:S], ACT.Exp, bias=gcol[:, h:h + 1])
                    ae.activation(c_dt[:, h, S:384], c_dt[:, h, S:384], ACT.Exp, bias=gcol[:, H + h:H + h + 1]).then_inc(gt_dt, 1)
                chunks(1, 5, (lambda j: c_lk[:, 2 + j, :], ACT.Copy, 1.0))
                for s in (6, 7):
                    chunks(1, s, (lambda j: c_lv[:, j, (s - 6) * PAIR:(s - 5) * PAIR], ACT.Copy, 1.0))
                chunks(1, 8, (lambda j: c_q[:, j, :], ACT.Copy, 1.0))
                for h in range(H):
                    ae.wait_ge(ml_h, h + 1)
                    ae.activation(c_h[:, h, :], acc[:, h, 0:S], ACT.Copy)
                    ae.activation(c_sq[:, h, :], acc[:, h, 0:S], ACT.Square).then_inc(ml_sq, 1)
                chunks(1, 9, (lambda j: c_q[:, 2 + j, :], ACT.Copy, 1.0))
                for h in range(H):
                    ae.wait_ge(ml_ar, h + 1)
                    own(ae.activation(c_rn[:, h, :], c_rn[:, h, :], ACT.Ln))
                    ae.activation(c_rn[:, h, :], c_rn[:, h, :], ACT.Exp, scale=-0.5).then_inc(ml_rs, 1)
                for s in (10, 11):
                    chunks(1, s, (lambda j: c_k[:, 2 * s - 20 + j, :], ACT.Copy, 1.0))
                y_split([(0, 2, 4), (2, 4, 5)])
                chunks(1, 12, (lambda j: c_v[:, j, 0:PAIR], ACT.Copy, 1.0))
                for h in range(H):
                    ae.wait_ge(mb_sm, h + 1)
                    ae.activation(c_p[:, h, 0:P], c_p[:, h, 0:P], ACT.Exp, bias=nmax[:, 2 * h:2 * h + 1],
                                  scale=P ** -0.5, accum_out=rsum[:, 2 * h:2 * h + 1])
                    ae.activation(c_p[:, h, P:384], c_p[:, h, P:384], ACT.Exp, bias=nmax[:, 2 * h + 1:2 * h + 2],
                                  scale=P ** -0.5, accum_out=rsum[:, 2 * h + 1:2 * h + 2]).then_inc(mb_p, 1)
                chunks(1, 13, (lambda j: c_v[:, j, PAIR:2 * PAIR], ACT.Copy, 1.0))
                ae.preload_act_table_set("silu_and_others")
                for h in range(H):
                    ae.wait_ge(mb_pt, h + 1)
                    ae.activation(c_pt[:, h, :], ch[:, h, 0:384], ACT.Copy).then_inc(mb_ptc, 1)
                after(1, 14)
                for p in range(2):
                    for h in (2 * p, 2 * p + 1):
                        ae.wait_ge(mb_o, h + 1)
                        ae.activation(act[:, 4 + h, :], ch[:, h, 0:S], ACT.Copy).then_inc(y_f, 1)
                    y_split([(4 + 2 * p, 6 + 2 * p, 7 + 2 * p)])
                for s in (15, 16):
                    after(1, s)

            loads()
            ae.preload_act_table_set("silu_and_others")
            ae.wait_ge(setup, 4)
            m = 0
            for kind, f in PHASES:
                norm(m)
                if m == 0:
                    for n in range(RING):
                        round_slot(n, 16)
                    small_loads()
                m += 1
                if kind == "ffn":
                    ffn(f)
                elif kind == "ab":
                    mixer_ab()
                else:
                    mixer_cd()
            norm(6)

        @block.vector
        def _(v):
            order = [0]

            def own(ins):
                order[0] += 1
                ins.then_inc(dve, 1)
                v.wait_ge(dve, order[0])

            def rest(n, pos):
                v.wait_ge(hi_done, n + 1)
                v.tensor_tensor(w_lo[:, pos, :], raw[:, pos, :], w_hi[:, pos, :].bitcast(F32), ALU.subtract).then_inc(lo_done, 1)

            def rest_half(n, pos, half):
                v.wait_ge(hi_done, n + 1)
                c = slice(half * SLOT // 2, (half + 1) * SLOT // 2)
                ins = v.tensor_tensor(w_lo[:, pos, c], raw[:, pos, c], w_hi[:, pos, c].bitcast(F32), ALU.subtract)
                if half:
                    ins.then_inc(lo_done, 1)

            def residual(m, scale, t):
                for half in range(2):
                    v.wait_ge(acc_done, 4 * (m - 1) + 2 * t + half + 1)
                    dst = xs[:, t, 512 * half:512 * half + 512]
                    v.scalar_tensor_tensor(out=dst, in0=acc[:, 2 * t + half, :], scalar=scale, in1=dst, op0=ALU.mult, op1=ALU.add).then_inc(x_ready, 1)

            def scaled(m, t):
                v.wait_ge(rstd_ready, 2 * m + t + 1)
                v.wait_ge(x_ready, 4 * m + 2 * t + 2)
                v.wait_ge(gains_in, 16 * (m + 1))
                for half in range(2):
                    c = slice(512 * half, 512 * half + 512)
                    v.scalar_tensor_tensor(out=xn[:, t, c], in0=xs[:, t, c], scalar=rstd[:, t:t + 1], in1=gains[:, c], op0=ALU.mult, op1=ALU.mult).then_inc(xn_ready, 1)

            def norm(m, scale):
                def low(b):
                    t, half = b // 2, b % 2
                    sl = (slice(None), slice(4 * half, 4 * half + 4), slice(t * P, (t + 1) * P))
                    v.wait_ge(xh_ready, 4 * m + b + 1)
                    tiles = ch[:, b, :].rearrange("p (k s) -> p k s", k=4)
                    v.tensor_tensor(x_lo[sl], tiles, x_hi[sl].bitcast(F32), ALU.subtract).then_inc(xl_ready, 1)

                n = FIRST_SLOT[m]
                if m:
                    rest_half(n, n % RING, 0)
                    residual(m, scale, 0)
                    rest_half(n, n % RING, 1)
                    residual(m, scale, 1)
                scaled(m, 0)
                scaled(m, 1)
                for b in range(4):
                    low(b)
                if m == 0:
                    rest(n, n % RING)
                rest(n + 1, (n + 1) % RING)
                if m == 0:
                    rest(2, 2)

            def ffn(f):
                def step(i, last=False, f_first=False):
                    q0 = 2 * ITER * f + 2 * i
                    n0 = FFN_BASE[f] + 3 * i

                    def hidden(j):
                        v.wait_ge(gate_silu, q0 + j + 1)
                        v.wait_ge(up_ready, q0 + j + 1)
                        v.tensor_tensor(act[:, j, :], ch[:, 2 * j + 1, 0:S], f_sig[:, j, :], ALU.mult).then_inc(hid, 1)
                        v.wait_ge(hid_hi, q0 + j + 1)
                        v.tensor_tensor(y_lo[:, j, :], act[:, j, :], y_hi[:, j, :].bitcast(F32), ALU.subtract).then_inc(hid_lo, 1)

                    if not f_first:
                        rest(n0 + 2, 2)
                    hidden(0)
                    hidden(1)
                    if not last:
                        rest(n0 + 3, 0)
                        rest(n0 + 4, 1)

                if f == 0:
                    step(0, f_first=True)
                with v.Fori(1 if f == 0 else 0, ITER - 1) as i:
                    step(i)
                step(ITER - 1, last=True)

            def after(m, s):
                n = MIX_BASE[m] + s + RING
                rest(n, n % RING)

            def sigmoid(buf):
                own(v.tensor_scalar(buf, buf, 1.0, None, ALU.add))
                own(v.reciprocal(buf, buf))

            def y_rest(parts):
                for k0, k1, count in parts:
                    v.wait_ge(y_h, count)
                    v.tensor_tensor(y_lo[:, k0:k1, :], act[:, k0:k1, :], y_hi[:, k0:k1, :].bitcast(F32), ALU.subtract).then_inc(y_l, 1)

            def mixer_ab():
                def forget(p):
                    h = slice(2 * p, 2 * p + 2)
                    v.wait_ge(chunk_out, 2 * p + 2)
                    own(v.tensor_scalar(b_f[:, h, :], b_f[:, h, :], 0.5, 0.5, ALU.mult, ALU.add))
                    for a in (2 * p, 2 * p + 1):
                        v.tensor_scalar(b_f[:, a, :], b_f[:, a, :], oml[:, a:a + 1], lb[:, a:a + 1], ALU.mult, ALU.add).then_inc(dve, 1)
                    order[0] += 2
                    v.wait_ge(dve, order[0])
                    v.tensor_scalar(b_kc[:, h, :], b_f[:, h, :], -1.0, 1.0, ALU.mult, ALU.add).then_inc(f_ready, 1)

                def cumulate(p):
                    h = slice(2 * p, 2 * p + 2)
                    v.wait_ge(lf_ready, p + 1)
                    for a in (2 * p, 2 * p + 1):
                        ins = v.tensor_tensor_scan(b_b[:, a, :], const("reset"), b_lf[:, a, :], 0.0, ALU.mult, ALU.add)
                        ins.then_inc(dve, 1)
                    order[0] += 2
                    v.wait_ge(dve, order[0])
                    for a in (2 * p, 2 * p + 1):
                        bb = b_b[:, a, :].rearrange("p (c s) -> p c s", s=HGC)
                        ins = v.tensor_tensor(b_lf[:, a, :].rearrange("p (c s) -> p c s", s=HGC),
                                              bb[:, :, HGC - 1:HGC].broadcast_to([P, S // HGC, HGC]), bb, ALU.subtract)
                    ins.then_inc(b_ready, 1)

                def keys(p):
                    h = slice(2 * p, 2 * p + 2)
                    v.wait_ge(e_ready, p + 1)
                    own(v.tensor_tensor(b_kd[:, h, :], b_kc[:, h, :], b_b[:, h, :], ALU.mult))
                    v.tensor_tensor(b_kc[:, h, :], b_kc[:, h, :], b_lf[:, h, :], ALU.mult).then_inc(kd_ready, 1)

                def queries(p):
                    h = slice(2 * p, 2 * p + 2)
                    v.wait_ge(chunk_out, 10 + 2 * p)
                    v.tensor_tensor(b_q[:, h, :], b_q[:, h, :], b_eb[:, h, :], ALU.mult).then_inc(q_ready, 1)

                def states(t):
                    v.wait_ge(hg_ds, t + 1)
                    for c in range(4 * t, min(4 * t + 4, 7)):
                        for h in range(H):
                            src = acc[:, c % 4, h * P:(h + 1) * P]
                            if c == 0:
                                ins = v.tensor_copy(b_s[:, 0, h, :], src)
                            else:
                                ins = v.scalar_tensor_tensor(out=b_s[:, c, h, :], in0=b_s[:, c - 1, h, :],
                                                             scalar=b_eb[:, h, c * HGC + HGC - 1:c * HGC + HGC], in1=src, op0=ALU.mult, op1=ALU.add)
                            ins.then_inc(dve, 1)
                        order[0] += H
                        v.wait_ge(dve, order[0])
                    v.sem_inc(hg_s, 1)

                def heads():
                    for h in range(H):
                        v.wait_ge(hg_rs, h + 1)
                        own(v.scalar_tensor_tensor(out=b_o[:, h, :], in0=b_o[:, h, :], scalar=gain(C_HGN + h), in1=b_rs[:, h, :], op0=ALU.mult, op1=ALU.mult))
                        ins = v.tensor_tensor(act[:, h, :], b_o[:, h, :], b_g[:, h, :], ALU.mult)
                    ins.then_inc(y_f, 1)

                v.wait_ge(prow_t, 1)
                own(v.tensor_copy(pcol[:, :], acc[:, 0, 0:N_ROWS]))
                lower_bound()
                v.wait_ge(const_in, 16)
                after(0, -1)
                forget(0)
                after(0, 0)
                forget(1)
                after(0, 1)
                for p in range(2):
                    cumulate(p)
                after(0, 2)
                for p in range(2):
                    keys(p)
                after(0, 3)
                after(0, 4)
                queries(0)
                after(0, 5)
                queries(1)
                after(0, 6)
                for h in range(H):
                    v.wait_ge(hg_at, h + 1)
                    v.tensor_copy(b_kt[:, h, :, :], acc[:, h, 0:S].rearrange("p (t d) -> p t d", t=T))
                    v.tensor_tensor(b_at[:, h, :, :], acc[:, h, S:2 * S].rearrange("p (t d) -> p t d", t=T),
                                    const("bd").unsqueeze(1).broadcast_to([P, T, P]), ALU.mult).then_inc(hg_ev, 1)
                after(0, 7)
                states(0)
                after(0, 8)
                states(1)
                after(0, 9)
                own(v.memset(b_z[:, :, 0:2], 0.0))
                for p in range(2):
                    after(0, 10 + p)
                    h = slice(2 * p, 2 * p + 2)
                    v.wait_ge(chunk_out, 22 + 2 * p)
                    own(v.tensor_tensor(b_z[:, h, 2:S + 2], b_c[:, h, :], b_u[:, h, :], ALU.mult))
                    if p == 0:
                        heads()
                    else:
                        y_rest([(0, 4, 1)])
                for w in (2, 1, 0):
                    for h in range(H):
                        if w == 2:
                            ins = v.tensor_scalar(b_c[:, h, :], b_z[:, h, 2:S + 2], gain(C_CW + 2 * H + h), gain(C_CB + h), ALU.mult, ALU.add)
                        else:
                            ins = v.scalar_tensor_tensor(out=b_c[:, h, :], in0=b_z[:, h, w:S + w], scalar=gain(C_CW + w * H + h), in1=b_c[:, h, :], op0=ALU.mult, op1=ALU.add)
                        ins.then_inc(dve, 1)
                    order[0] += H
                    v.wait_ge(dve, order[0])
                for p in range(2):
                    h = slice(2 * p, 2 * p + 2)
                    v.wait_ge(chunk_out, 26 + 2 * p)
                    v.tensor_tensor(act[:, 4 + 2 * p:6 + 2 * p, :], b_c[:, h, :], b_bg[:, h, :], ALU.mult).then_inc(y_f, 1)
                    y_rest([(4 + 2 * p, 6 + 2 * p, 2 + p)])
                    after(0, 12 + p)
                after(0, 14)

            def mixer_cd():
                after(1, -1)
                v.wait_ge(gt_mm, 1)
                v.wait_ge(gate_in, 48)
                v.tensor_scalar(row[:, 0, :], acc[0:H, 0, 0:S], gbias[:, 0:1], None, ALU.add)
                own(v.tensor_scalar(row[:, 1, :], acc[32:32 + H, 0, 0:S], gbias[:, 1:2], None, ALU.add))
                v.scalar_tensor_tensor(out=row[:, 2, :], in0=row[:, 1, :], scalar=-1.0, in1=row[:, 1, :], op0=ALU.mult, op1=ALU.min).then_inc(gt_na, 1)
                after(1, 0)
                after(1, 1)
                v.wait_ge(gt_ln, 1)
                own(v.scalar_tensor_tensor(out=row[:, 1, :], in0=row[:, 1, :], scalar=0.0, in1=row[:, 3, :], op0=ALU.min, op1=ALU.subtract))
                one_row = const("ones")[0:H, 0:1].broadcast_to([H, S])
                own(v.tensor_tensor_scan(row[:, 4, :], one_row, row[:, 1, :], 0.0, ALU.mult, ALU.add))
                own(v.tensor_tensor(row[:, 5, :], row[:, 0, :], row[:, 4, :], ALU.subtract))
                own(v.tensor_tensor_scan(row[:, 2, :], one_row, row[:, 5, :], 0.0, ALU.mult, ALU.max))
                own(v.tensor_scalar(row[:, 6, :], row[:, 2, :], -1.0, None, ALU.mult))
                v.tensor_tensor(row[:, 7, :], row[:, 6, :], row[:, 4, :], ALU.subtract).then_inc(gt_rows, 1)
                v.tensor_scalar(c_oe[:, :, :], c_oe[:, :, :], 0.5, 0.5, ALU.mult, ALU.add).then_inc(dve, 1)
                order[0] += 1
                after(1, 2)
                v.wait_ge(gt_tp, 1)
                v.tensor_copy(gcol, acc[:, 0, 0:2 * H]).then_inc(gt_col, 1)
                after(1, 3)
                after(1, 4)
                for h in range(H):
                    v.wait_ge(gt_bc, h + 1)
                    v.tensor_tensor(c_dt[:, h, 0:S], acc[:, h, 0:S], const("m_ji")[:, 0:S], ALU.add)
                    v.tensor_tensor(c_dt[:, h, S:384], acc[:, h, P:S], const("m_ji")[:, S:384], ALU.add).then_inc(gt_pre, 1)
                for s in (5, 6):
                    after(1, s)
                for h in range(H):
                    v.wait_ge(ml_s, h + 1)
                    v.wait_ge(gt_dt, h + 1)
                    v.tensor_tensor(c_dt[:, h, :], acc[:, h, 0:384], c_dt[:, h, :], ALU.mult).then_inc(ml_w, 1)
                for s in (7, 8):
                    after(1, s)
                for h in range(H):
                    v.wait_ge(ml_n, h + 1)
                    own(v.tensor_tensor(c_em[:, h, :], acc[:, h, S:2 * S], c_em[:, h, :], ALU.max))
                    own(v.scalar_tensor_tensor(out=c_em[:, h, :], in0=acc[:, h, S:2 * S], scalar=-1.0, in1=c_em[:, h, :], op0=ALU.mult, op1=ALU.max))
                    v.scalar_tensor_tensor(out=c_em[:, h, :], in0=c_em[:, h, :], scalar=EPS, in1=c_em[:, h, :], op0=ALU.mult, op1=ALU.mult).then_inc(ml_h, 1)
                after(1, 9)
                v.wait_ge(ml_h, H)
                for h in range(H):
                    v.wait_ge(ml_ss, h + 1)
                    v.scalar_tensor_tensor(out=c_rn[:, h, :], in0=acc[:, h, 0:S], scalar=1.0 / P, in1=c_em[:, h, :], op0=ALU.mult, op1=ALU.add).then_inc(ml_ar, 1)
                after(1, 10)
                for h in range(H):
                    v.wait_ge(ml_rs, h + 1)
                    own(v.scalar_tensor_tensor(out=c_h[:, h, :], in0=c_h[:, h, :], scalar=gain(C_MLN + h), in1=c_rn[:, h, :], op0=ALU.mult, op1=ALU.mult))
                    ins = v.tensor_tensor(act[:, h, :], c_h[:, h, :], c_oe[:, h, :], ALU.mult)
                    if h % 2:
                        ins.then_inc(y_f, 1)
                sin = const("sin").unsqueeze(1).broadcast_to([P, 2, S])

                def rotary(n, buf):
                    for half in range(2):
                        v.wait_ge(mb_rot, 2 * n + half + 1)
                        ins = v.tensor_tensor(c_rs[:, n, 512 * half:512 * half + 512].rearrange("p (h s) -> p h s", h=2),
                                              acc[:, 2 * n + half, :].rearrange("p (h s) -> p h s", h=2), sin, ALU.mult)
                        ins.then_inc(dve, 1)
                    order[0] += 2
                    v.wait_ge(dve, order[0])
                    v.wait_ge(mb_cos, n + 1)
                    v.tensor_tensor(buf[:, :, :], buf[:, :, :], c_rs[:, n, :].rearrange("p (h s) -> p h s", h=H), ALU.add).then_inc(mb_qk, 1)

                rotary(0, c_q)
                rotary(1, c_k)
                after(1, 11)
                y_rest([(0, 2, 4), (2, 4, 5)])
                v.wait_ge(mb_qk, 2)
                for h in range(H):
                    v.wait_ge(mb_s, h + 1)
                    own(v.tensor_tensor(c_p[:, h, :], acc[:, h, 0:384], const("m_ij"), ALU.add))
                    v.tensor_reduce(nmax[:, 2 * h:2 * h + 1], c_p[:, h, 0:P], AX.X, ALU.max)
                    own(v.tensor_reduce(nmax[:, 2 * h + 1:2 * h + 2], c_p[:, h, P:384], AX.X, ALU.max))
                    v.tensor_scalar(nmax[:, 2 * h:2 * h + 2], nmax[:, 2 * h:2 * h + 2], -(P ** -0.5), None, ALU.mult).then_inc(mb_sm, 1)
                after(1, 12)
                for h in range(H):
                    v.wait_ge(mb_p, h + 1)
                    own(v.reciprocal(rsum[:, 2 * h:2 * h + 2], rsum[:, 2 * h:2 * h + 2]))
                    v.tensor_scalar(c_p[:, h, 0:P], c_p[:, h, 0:P], rsum[:, 2 * h:2 * h + 1], None, ALU.mult)
                    v.tensor_scalar(c_p[:, h, P:384], c_p[:, h, P:384], rsum[:, 2 * h + 1:2 * h + 2], None, ALU.mult).then_inc(mb_pn, 1)
                after(1, 13)
                after(1, 14)
                y_rest([(4, 6, 6), (6, 8, 7)])

            for t in range(T):
                v.wait_ge(x_in[t], 16)
                v.sem_inc(x_ready, 2)

            def lower_bound():
                rows = pcol[:, C_LB:C_LB + 12].rearrange("p (r h) -> p r h", r=3)
                own(v.tensor_tensor(lbt, rows[:, 0, :], rows[:, 1, :], ALU.max))
                own(v.tensor_tensor(lbt, lbt, rows[:, 2, :], ALU.max))
                e = lbe.rearrange("p (r h) -> p r h", r=3)
                v.tensor_tensor(e, rows, lbt.unsqueeze(1).broadcast_to([P, 3, H]), ALU.subtract).then_inc(lb_sub, 1)
                v.wait_ge(lb_exp, 1)
                own(v.tensor_tensor(lbt, e[:, 0, :], e[:, 1, :], ALU.add))
                own(v.tensor_tensor(lbt, lbt, e[:, 2, :], ALU.add))
                own(v.reciprocal(lbt, lbt))
                own(v.tensor_tensor(lb, e[:, 0, :], lbt, ALU.mult))
                own(v.tensor_scalar(oml, lb, -1.0, 1.0, ALU.mult, ALU.add))

            scale = 1.0
            m = 0
            for kind, f in PHASES:
                norm(m, scale)
                m += 1
                if kind == "ffn":
                    ffn(f)
                elif kind == "ab":
                    mixer_ab()
                else:
                    mixer_cd()
                scale = 0.5 if kind == "ffn" else 1.0
            for t in range(T):
                residual(6, scale, t)
            for t in range(T):
                scaled(6, t)

        @block.tensor
        def _(pe):
            def three(dst, l_hi, l_lo, r_hi, r_lo, start, stop):
                pe.matmul(dst, l_hi, r_hi, start=start, stop=False, skip_group_check=True)
                pe.matmul(dst, l_hi, r_lo, start=False, stop=False, skip_group_check=True)
                return pe.matmul(dst, l_lo, r_hi, start=False, stop=stop, skip_group_check=True)

            def channels(dst, pos, j):
                c = slice(j * P, (j + 1) * P)
                for k in range(KD):
                    ins = three(dst, slot3(w_hi, pos)[:, k, c], slot3(w_lo, pos)[:, k, c], x_hi[:, k, :], x_lo[:, k, :], k == 0, k == KD - 1)
                return ins

            def tokens(dst, pos, t):
                c = slice(t * P, (t + 1) * P)
                for k in range(KD):
                    ins = three(dst, x_hi[:, k, c], x_lo[:, k, c], slot3(w_hi, pos)[:, k, :], slot3(w_lo, pos)[:, k, :], k == 0, k == KD - 1)
                return ins

            def part(pos, t, half, r, k, start, stop):
                c, w = slice(t * P, (t + 1) * P), slice(512 * half, 512 * half + 512)
                return three(acc[:, 2 * t + half, :], y_hi[:, k, c], y_lo[:, k, c], slot2(w_hi, pos)[:, r, w], slot2(w_lo, pos)[:, r, w], start, stop)

            def project(pos, rows, start, done, split=None):
                if not done:
                    for t in range(T):
                        for r, k in rows:
                            for half in range(2):
                                ins = part(pos, t, half, r, k, start and r == 0, False)
                    return ins
                for t in range(T):
                    for half, (r, k) in ([(0, rows[0]), (1, rows[0]), (0, rows[1]), (1, rows[1])] if t == 0 else
                                         [(0, rows[0]), (0, rows[1]), (1, rows[0]), (1, rows[1])]):
                        if split is not None and t == 0:
                            pe.wait_ge(hid_lo, split + r + 1)
                        ins = part(pos, t, half, r, k, start and r == 0, r == 1)
                        if r == 1:
                            ins.then_inc(acc_done, 1)

            def norm(m):
                for t in range(T):
                    for half in range(2):
                        pe.wait_ge(xn_ready, 4 * m + 2 * t + half + 1)
                        for k in range(4):
                            ins = pe.transpose(ch[:, 2 * t + half, k * P:(k + 1) * P], xn[:, t, (4 * half + k) * P:(4 * half + k + 1) * P], ident)
                        ins.then_inc(tp_ready, 1)
                if m == 1:
                    pe.wait_ge(small_in, 5 * 16)
                    pe.wait_ge(x_ready, 4 * m + 4)
                    pe.transpose(acc[:, 0, 0:N_ROWS], prow[0:N_ROWS, :], ident[0:N_ROWS, 0:N_ROWS]).then_inc(prow_t, 1)
                pe.wait_ge(xl_ready, 4 * m + 4)

            def ffn(f):
                def step(i, last=False):
                    q0 = 2 * ITER * f + 2 * i
                    n0 = FFN_BASE[f] + 3 * i
                    for j in range(2):
                        if j == 0:
                            pe.wait_ge(lo_done, n0 + 1)
                        channels(ch[:, 2 * j, 0:S], 0, j).then_inc(gate_ready, 1)
                        if j == 0:
                            pe.wait_ge(lo_done, n0 + 2)
                        channels(ch[:, 2 * j + 1, 0:S], 1, j).then_inc(up_ready, 1)
                    pe.wait_ge(lo_done, n0 + 3)
                    if last:
                        project(2, [(0, 0), (1, 1)], False, True, split=q0)
                    else:
                        for j in range(2):
                            pe.wait_ge(hid_lo, q0 + j + 1)
                            ins = project(2, [(j, j)], False, False)
                        ins.then_inc(out_used, 1)

                for b in range(4):
                    pe.matmul(acc[:, b, :], zb[:, 0:P], zb[:, :], start=True, stop=False, skip_group_check=True)
                step(0)
                with pe.Fori(1, ITER - 1) as i:
                    step(i)
                step(ITER - 1, last=True)

            def slot(m, s):
                n = MIX_BASE[m] + s
                pe.wait_ge(lo_done, n + 1)
                for j in range(2):
                    c = 2 * s + j
                    if c >= 4:
                        pe.wait_ge(chunk_out, CHUNKS * m + c - 3)
                    dst = ch[:, c % 4, 0:S]
                    if s in TOK[m]:
                        ins = tokens(dst, n % RING, j)
                    else:
                        ins = channels(dst, n % RING, j)
                    ins.then_inc(chunk, 1)

            def out_slot(m, s, y_count):
                n = MIX_BASE[m] + 14 + s
                pe.wait_ge(lo_done, n + 1)
                pe.wait_ge(y_l, y_count)
                k0 = (AB_ROWS, CD_ROWS)[m][s]
                ins = project(n % RING, [(0, k0), (1, k0 + 1)], s == 0, s == 3)
                if s < 3:
                    ins.then_inc(out_used, 1)

            def mixer_ab():
                for s in range(7):
                    slot(0, s)
                pe.wait_ge(kd_ready, 2)
                pe.wait_ge(q_ready, 2)
                for h in range(H):
                    for t in range(T):
                        pe.transpose(acc[:, h, t * P:(t + 1) * P], b_kc[:, h, t * P:(t + 1) * P], ident)
                    for t in range(T):
                        c = slice(t * P, (t + 1) * P)
                        ins = pe.matmul(acc[:, h, S + t * P:S + (t + 1) * P], b_kd[:, h, c], b_q[:, h, c], start=True, stop=True)
                    ins.then_inc(hg_at, 1)
                slot(0, 7)
                pe.wait_ge(hg_ev, H)
                pe.wait_ge(chunk_out, 8)
                for t in range(T):
                    if t:
                        slot(0, 8)
                        pe.wait_ge(hg_s, 1)
                    for c in range(4 if t == 0 else 3):
                        r = slice(HGC * c, HGC * (c + 1))
                        for h in range(H):
                            ins = pe.matmul(acc[:, c, h * P:(h + 1) * P], b_kt[r, h, t, :], b_v[r, t, h * P:(h + 1) * P], start=True, stop=True)
                    ins.then_inc(hg_ds, 1)
                slot(0, 9)
                pe.wait_ge(hg_s, 2)
                for h in range(H):
                    for t in range(T):
                        pe.matmul(acc[:, h, t * P:(t + 1) * P], b_v[:, t, h * P:(h + 1) * P], b_at[:, h, t, :], start=True, stop=False, skip_group_check=True)
                        for c in range(max(4 * t, 1), 4 * t + 4):
                            s = slice(c * HGC, (c + 1) * HGC)
                            ins = pe.matmul(acc[:, h, s], b_s[:, c - 1, h, :], b_q[:, h, s], start=False, stop=(c == 4 * t + 3), skip_group_check=True)
                    ins.then_inc(hg_o, 1)
                slot(0, 10)
                for h in range(H):
                    pe.wait_ge(hg_oc, h + 1)
                    pe.matmul(acc[:, h, 0:S], ones, b_sq[:, h, :], start=True, stop=True).then_inc(hg_ss, 1)
                for s in (11, 12, 13):
                    slot(0, s)
                pe.wait_ge(hg_rs, H)
                for s, count in enumerate((1, 1, 2, 3)):
                    out_slot(0, s, count)

            def mixer_cd():
                slot(1, 0)
                pe.wait_ge(gate_in, 48)
                pe.wait_ge(xt_ready, 1)
                for k in range(KD):
                    ins = pe.matmul(acc[0:36, 0, 0:S], wgate[:, k, :], act[:, k, :], start=(k == 0), stop=(k == KD - 1))
                ins.then_inc(gt_mm, 1)
                for s in (1, 2, 3):
                    slot(1, s)
                pe.wait_ge(gt_rows, 1)
                for t in range(T):
                    ins = pe.transpose(acc[:, 0, t * H:(t + 1) * H], row[:, 5, t * P:(t + 1) * P], ident[0:H, 0:H])
                ins.then_inc(gt_tp, 1)
                slot(1, 4)
                pe.wait_ge(gt_col, 1)
                sel = const("sel").rearrange("p (h m) -> p h m", h=H)
                for h in range(H):
                    pe.matmul(acc[:, h, :], sel[0:H, h, :], row[:, 6:8, :].rearrange("p n s -> p (n s)"), start=True, stop=True).then_inc(gt_bc, 1)
                for s in (5, 6):
                    slot(1, s)
                pe.wait_ge(gt_dt, H)
                pe.wait_ge(chunk_out, CHUNKS + 12)
                for h in range(H):
                    pe.matmul(acc[:, h, 0:S], c_lk[:, h, 0:P], c_lq[:, h, :], start=True, stop=True)
                    pe.matmul(acc[:, h, S:384], c_lk[:, h, P:S], c_lq[:, h, P:S], start=True, stop=True).then_inc(ml_s, 1)
                slot(1, 7)
                slot(1, 8)
                pe.wait_ge(chunk_out, CHUNKS + 16)
                for h in range(H):
                    pe.wait_ge(ml_w, h + 1)
                    g = slice(h * P, (h + 1) * P)
                    for lhs, at in (((c_lv[:, 0, g], c_lv[:, 1, g]), 0), ((ones, ones), S)):
                        pe.matmul(acc[:, h, at:at + S], lhs[0], c_dt[:, h, 0:S], start=True, stop=False, skip_group_check=True)
                        ins = pe.matmul(acc[:, h, at + P:at + S], lhs[1], c_dt[:, h, S:384], start=False, stop=True, skip_group_check=True)
                    ins.then_inc(ml_n, 1)
                slot(1, 9)
                for h in range(H):
                    pe.wait_ge(ml_sq, h + 1)
                    pe.matmul(acc[:, h, 0:S], ones, c_sq[:, h, :], start=True, stop=True).then_inc(ml_ss, 1)
                slot(1, 10)

                def rotate(n, buf, moved):
                    for half in range(2):
                        pe.wait_ge(chunk_out, CHUNKS + moved + 2 * half)
                        pe.matmul(acc[:, 2 * n + half, :], const("rot"), buf[:, 2 * half:2 * half + 2, :].rearrange("p h s -> p (h s)"),
                                  start=True, stop=True).then_inc(mb_rot, 1)

                pe.wait_ge(ml_ar, H)
                rotate(0, c_q, 18)
                slot(1, 11)
                rotate(1, c_k, 22)
                slot(1, 12)
                pe.wait_ge(mb_qk, 2)
                for h in range(H):
                    pe.matmul(acc[:, h, 0:P], c_q[:, h, 0:P], c_k[:, h, 0:P], start=True, stop=True)
                    pe.matmul(acc[:, h, P:384], c_q[:, h, P:S], c_k[:, h, :], start=True, stop=True).then_inc(mb_s, 1)
                slot(1, 13)
                pe.wait_ge(mb_sm, H)
                pe.wait_ge(chunk_out, 2 * CHUNKS)
                for h in range(H):
                    pe.wait_ge(mb_pn, h + 1)
                    for b in range(3):
                        ins = pe.transpose(ch[:, h, b * P:(b + 1) * P], c_p[:, h, b * P:(b + 1) * P], ident)
                    ins.then_inc(mb_pt, 1)
                out_slot(1, 0, 4)
                for h in range(H):
                    pe.wait_ge(mb_ptc, h + 1)
                    g = slice(h * P, (h + 1) * P)
                    pe.matmul(ch[:, h, 0:S], c_v[:, 0, g], c_pt[:, h, 0:S], start=True, stop=False, skip_group_check=True)
                    pe.matmul(ch[:, h, P:S], c_v[:, 1, g], c_pt[:, h, S:384], start=False, stop=True, skip_group_check=True).then_inc(mb_o, 1)
                for s, count in ((1, 5), (2, 6), (3, 7)):
                    out_slot(1, s, count)

            pe.wait_ge(ident_in, 16)
            pe.wait_ge(setup, 5)
            m = 0
            for kind, f in PHASES:
                norm(m)
                if kind == "ffn":
                    if m:
                        pe.wait_ge(x_ready, 4 * m + 4)
                m += 1
                if kind == "ffn":
                    ffn(f)
                elif kind == "ab":
                    pe.wait_ge(const_in, 16)
                    mixer_ab()
                else:
                    mixer_cd()


_INS = ["x", "ffn_norm", "ffn_w_in", "ffn_w_out", "mix_norm", "ab_w_in", "ab_w_out", "hgrn_lb_logits", "hgrn_out_norm",
        "conv_w", "conv_b", "cd_w_in", "cd_w_out", "mlstm_gate_bias", "mlstm_out_norm", "final_norm"]


def kernel(**inputs):
    import concourse.bacc as bacc
    from concourse.bass_utils import run_bass_kernel_spmd

    nc = bacc.Bacc("TRN2", target_bir_lowering=False, num_devices=1)
    arrays = {f"in_{n}": np.ascontiguousarray(inputs[n]) for n in _INS}
    arrays["in_consts"] = shape_constants()
    args = [nc.dram_tensor(n, a.shape, mybir.dt.from_np(a.dtype), kind="ExternalInput").ap() for n, a in arrays.items()]
    args.append(nc.dram_tensor("out_0", (1, S, D), F32, kind="ExternalOutput").ap())
    build(nc, *args)
    r = run_bass_kernel_spmd(nc, [arrays], core_ids=[0])
    return r.results[0]["out_0"]
```
